# Optimizing a Trainium2 kernel written in Bass

```python
import math
import jax, jax.numpy as jnp
from jax import lax
import numpy as np

D_MODEL = 2048
BATCH = 1
SEQ = 256
DEPTH = 2

N_A_LAYERS = DEPTH // 2
N_B_LAYERS = DEPTH - N_A_LAYERS
MEM_LEN = 256
MEM_HEADS = 4
MEM_HEAD_DIM = 128
MEM_WIDTH = MEM_HEADS * MEM_HEAD_DIM
MIX_WIDTH = D_MODEL
POOL_WIDTH = MIX_WIDTH - MEM_WIDTH
POOL_WINDOWS = (2, 4, 8, 16)
N_POOL_GROUPS = len(POOL_WINDOWS)
POOL_GROUP = POOL_WIDTH // N_POOL_GROUPS
DIFF_HEAD_DIM = 64
DIFF_V_DIM = 2 * DIFF_HEAD_DIM
DIFF_HEADS = POOL_WIDTH // DIFF_V_DIM
DIFF_QK_WIDTH = DIFF_HEADS * DIFF_HEAD_DIM
DIFF_V_WIDTH = DIFF_HEADS * DIFF_V_DIM
KV_WIDTH = 2 * DIFF_QK_WIDTH + DIFF_V_WIDTH
ROPE_THETA = 500000.0
ROPE_DIM = DIFF_HEAD_DIM // 4
D_FF = 4 * D_MODEL
Q_BLOCK = 128
EPS = 1e-6
NEG_INF = -1e30


def rms_norm(x, g):
    xf = x.astype(jnp.float32)
    y = xf * lax.rsqrt(jnp.mean(xf * xf, axis=-1, keepdims=True) + EPS)
    return (y * g.astype(jnp.float32)).astype(x.dtype)

def rope_tables(seq):
    pos = jnp.arange(seq, dtype=jnp.float32)
    inv = ROPE_THETA ** (-(jnp.arange(ROPE_DIM // 2, dtype=jnp.float32) * 2.0) / ROPE_DIM)
    ang = pos[:, None] * inv[None, :]
    return jnp.cos(ang), jnp.sin(ang)

def partial_rope(t, cos, sin):
    half = ROPE_DIM // 2
    c = cos[None, :, None, :].astype(t.dtype)
    s = sin[None, :, None, :].astype(t.dtype)
    r1, r2, rest = t[..., :half], t[..., half:ROPE_DIM], t[..., ROPE_DIM:]
    return jnp.concatenate([r1 * c - r2 * s, r1 * s + r2 * c, rest], axis=-1)

def causal_multiscale_pool(u):
    B, S, _ = u.shape
    groups = u.astype(jnp.float32).reshape(B, S, N_POOL_GROUPS, POOL_GROUP)
    csum = jnp.cumsum(groups, axis=1)
    t = jnp.arange(S)
    outs = []
    for g, w in enumerate(POOL_WINDOWS):
        cg = csum[:, :, g]
        lag = jnp.pad(cg, ((0, 0), (w, 0), (0, 0)))[:, :S]
        count = jnp.minimum(t + 1, w).astype(jnp.float32)[None, :, None]
        outs.append((cg - lag) / count)
    mean = jnp.stack(outs, axis=2)
    return (mean - groups).astype(u.dtype)

def memory_cross_attention(q, mem, mem_norm_g, w_mem_kv, mq_g, mk_g):
    B, S, _ = q.shape
    M = mem.shape[1]
    mkv = rms_norm(mem, mem_norm_g) @ w_mem_kv
    k = mkv[..., :MEM_WIDTH].reshape(B, M, MEM_HEADS, MEM_HEAD_DIM)
    v = mkv[..., MEM_WIDTH:].reshape(B, M, MEM_HEADS, MEM_HEAD_DIM)
    q = rms_norm(q.reshape(B, S, MEM_HEADS, MEM_HEAD_DIM), mq_g)
    k = rms_norm(k, mk_g)
    s = jnp.einsum('bqhd,bkhd->bhqk', q, k).astype(jnp.float32) * (MEM_HEAD_DIM ** -0.5)
    p = jax.nn.softmax(s, axis=-1).astype(v.dtype)
    o = jnp.einsum('bhqk,bkhd->bqhd', p, v)
    return o.reshape(B, S, MEM_WIDTH)

def differential_attention(q1, q2, k1, k2, v, lam):
    B, S, H, dk = q1.shape
    dv = v.shape[-1]
    nb = S // Q_BLOCK
    scale = dk ** -0.5
    key_pos = jnp.arange(S)

    def blockify(t):
        return t.reshape(B, nb, Q_BLOCK, H, dk).transpose(1, 0, 2, 3, 4)

    def one_block(args):
        q1b, q2b, start = args
        q_pos = start + jnp.arange(Q_BLOCK)
        mask = key_pos[None, :] <= q_pos[:, None]

        def probs(qb, k):
            s = jnp.einsum('bqhd,bkhd->bhqk', qb, k).astype(jnp.float32) * scale
            return jax.nn.softmax(jnp.where(mask, s, NEG_INF), axis=-1)

        a = probs(q1b, k1) - lam * probs(q2b, k2)
        return jnp.einsum('bhqk,bkhd->bqhd', a.astype(v.dtype), v)

    starts = jnp.arange(nb) * Q_BLOCK
    out = lax.map(one_block, (blockify(q1), blockify(q2), starts))
    return out.transpose(1, 0, 2, 3, 4).reshape(B, S, H, dv)

def shared_kv(x, kv_norm, w_kv, k_norm, cos, sin):
    B, S, _ = x.shape
    kv = rms_norm(x, kv_norm) @ w_kv
    k1 = kv[..., :DIFF_QK_WIDTH].reshape(B, S, DIFF_HEADS, DIFF_HEAD_DIM)
    k2 = kv[..., DIFF_QK_WIDTH:2 * DIFF_QK_WIDTH].reshape(B, S, DIFF_HEADS, DIFF_HEAD_DIM)
    v = kv[..., 2 * DIFF_QK_WIDTH:].reshape(B, S, DIFF_HEADS, DIFF_V_DIM)
    k1 = partial_rope(rms_norm(k1, k_norm), cos, sin)
    k2 = partial_rope(rms_norm(k2, k_norm), cos, sin)
    return k1, k2, v

def squared_relu_mlp(h, w1, w2):
    z = jax.nn.relu(h @ w1)
    return (z * z) @ w2

def first_inputs(seed: int = 0) -> dict:
    key = jax.random.key(seed)
    ks = jax.random.split(key, 20)
    f32 = jnp.float32

    def nrm(k, shape, scale):
        return jax.random.normal(k, shape, f32) * scale

    def gain(k, shape, noise=0.02):
        return 1.0 + noise * jax.random.normal(k, shape, f32)

    return {
        'x': nrm(ks[0], (BATCH, SEQ, D_MODEL), 1.0),
        'mem': nrm(ks[1], (BATCH, MEM_LEN, D_MODEL), 1.0),
        'mix_norm': gain(ks[2], (DEPTH, D_MODEL)),
        'w_in': nrm(ks[3], (DEPTH, D_MODEL, MIX_WIDTH), D_MODEL ** -0.5),
        'w_out': nrm(ks[4], (DEPTH, MIX_WIDTH, D_MODEL), 0.5 * MIX_WIDTH ** -0.5),
        'mem_norm': gain(ks[5], (DEPTH, D_MODEL)),
        'w_mem_kv': nrm(ks[6], (DEPTH, D_MODEL, 2 * MEM_WIDTH), D_MODEL ** -0.5),
        'mem_q_norm': gain(ks[7], (DEPTH, MEM_HEAD_DIM)),
        'mem_k_norm': gain(ks[8], (DEPTH, MEM_HEAD_DIM)),
        'ffn_norm': gain(ks[9], (DEPTH, D_MODEL)),
        'w_ff1': nrm(ks[10], (DEPTH, D_MODEL, D_FF), D_MODEL ** -0.5),
        'w_ff2': nrm(ks[11], (DEPTH, D_FF, D_MODEL), 0.5 * D_FF ** -0.5),
        'pool_w': nrm(ks[12], (N_A_LAYERS, N_POOL_GROUPS, POOL_GROUP, POOL_GROUP), POOL_GROUP ** -0.5),
        'pool_scale': gain(ks[13], (N_A_LAYERS, POOL_WIDTH), 0.1),
        'kv_norm': gain(ks[14], (D_MODEL,)),
        'w_kv': nrm(ks[15], (D_MODEL, KV_WIDTH), D_MODEL ** -0.5),
        'k_norm': gain(ks[16], (DIFF_HEAD_DIM,)),
        'q_norm': gain(ks[17], (N_B_LAYERS, DIFF_HEAD_DIM)),
        'diff_lambda': nrm(ks[18], (N_B_LAYERS, 4, DIFF_HEAD_DIM), 0.1),
        'subln_norm': gain(ks[19], (N_B_LAYERS, DIFF_V_DIM)),
    }

def first_block(x, mem, mix_norm, w_in, w_out, mem_norm, w_mem_kv, mem_q_norm, mem_k_norm,
              ffn_norm, w_ff1, w_ff2, pool_w, pool_scale, kv_norm, w_kv, k_norm, q_norm,
              diff_lambda, subln_norm):
    B, S, _ = x.shape
    cos, sin = rope_tables(S)
    sk1 = sk2 = sv = None
    for i in range(DEPTH):
        if i == N_A_LAYERS:
            sk1, sk2, sv = shared_kv(x, kv_norm, w_kv, k_norm, cos, sin)
        u = rms_norm(x, mix_norm[i]) @ w_in[i]
        if i < N_A_LAYERS:
            a = i
            pooled = causal_multiscale_pool(u[..., :POOL_WIDTH])
            token_out = jnp.einsum('bsgc,gcd->bsgd', pooled, pool_w[a]).reshape(B, S, POOL_WIDTH) * pool_scale[a]
            mem_q = u[..., POOL_WIDTH:]
        else:
            b = i - N_A_LAYERS
            lam_init = 0.8 - 0.6 * math.exp(-0.3 * i)
            q1 = u[..., :DIFF_QK_WIDTH].reshape(B, S, DIFF_HEADS, DIFF_HEAD_DIM)
            q2 = u[..., DIFF_QK_WIDTH:2 * DIFF_QK_WIDTH].reshape(B, S, DIFF_HEADS, DIFF_HEAD_DIM)
            q1 = partial_rope(rms_norm(q1, q_norm[b]), cos, sin)
            q2 = partial_rope(rms_norm(q2, q_norm[b]), cos, sin)
            lq = diff_lambda[b].astype(jnp.float32)
            lam = jnp.exp(jnp.sum(lq[0] * lq[1])) - jnp.exp(jnp.sum(lq[2] * lq[3])) + lam_init
            o = differential_attention(q1, q2, sk1, sk2, sv, lam)
            token_out = (rms_norm(o, subln_norm[b]) * (1.0 - lam_init)).reshape(B, S, DIFF_V_WIDTH)
            mem_q = u[..., 2 * DIFF_QK_WIDTH:]
        mem_out = memory_cross_attention(mem_q, mem, mem_norm[i], w_mem_kv[i], mem_q_norm[i], mem_k_norm[i])
        x = x + jnp.concatenate([token_out, mem_out], axis=-1) @ w_out[i]
        x = x + squared_relu_mlp(rms_norm(x, ffn_norm[i]), w_ff1[i], w_ff2[i])
    return x


DEPTH_2 = 1

LRU_WIDTH = D_MODEL
LRU_BLOCKS = 16
LRU_BLOCK_DIM = LRU_WIDTH // LRU_BLOCKS
LRU_C = 8.0
CONV_WIDTH = 4
CONV_LEFT = 2
N_HEADS = 16
N_KV_HEADS = 4
HEAD_DIM = 128
GROUP = N_HEADS // N_KV_HEADS
ATTN_WIDTH = N_HEADS * HEAD_DIM
KV_WIDTH_2 = N_KV_HEADS * HEAD_DIM
WINDOW = 128
BLOCK = 128
ROT_DIM = HEAD_DIM // 4
NORM_EPS = 1e-6
IN_SPLITS = (LRU_WIDTH, LRU_WIDTH, ATTN_WIDTH, KV_WIDTH_2, KV_WIDTH_2, ATTN_WIDTH, D_MODEL, D_MODEL)
IN_WIDTH = sum(IN_SPLITS)


def rms_norm_2(x, w):
    xf = x.astype(jnp.float32)
    y = xf * lax.rsqrt(jnp.mean(xf * xf, axis=-1, keepdims=True) + NORM_EPS)
    return (y * w.astype(jnp.float32)).astype(x.dtype)

def centred_depthwise_conv(u, w, b):
    s = u.shape[1]
    up = jnp.pad(u, ((0, 0), (CONV_LEFT, CONV_WIDTH - 1 - CONV_LEFT), (0, 0)))
    y = b
    for tap in range(CONV_WIDTH):
        y = y + up[:, tap:tap + s] * w[tap]
    return y

def _linear_combine(e1, e2):
    a1, b1 = e1
    a2, b2 = e2
    return a1 * a2, a2 * b1 + b2

def rg_lru(u, w_r, b_r, w_i, b_i, lam, reverse):
    bsz, s, _ = u.shape
    ub = u.reshape(bsz, s, LRU_BLOCKS, LRU_BLOCK_DIM)
    gate_r = jax.nn.sigmoid(jnp.einsum('bsni,nij->bsnj', ub, w_r).reshape(bsz, s, LRU_WIDTH) + b_r)
    gate_i = jax.nn.sigmoid(jnp.einsum('bsni,nij->bsnj', ub, w_i).reshape(bsz, s, LRU_WIDTH) + b_i)
    log_a = -LRU_C * gate_r.astype(jnp.float32) * jax.nn.softplus(-lam.astype(jnp.float32))
    a = jnp.exp(log_a)
    in_scale = jnp.sqrt(-jnp.expm1(2.0 * log_a))
    b = in_scale * (gate_i * u).astype(jnp.float32)
    _, h = lax.associative_scan(_linear_combine, (a, b), axis=1, reverse=reverse)
    return h

def partial_rope_2(t, cos, sin):
    half = ROT_DIM // 2
    tf = t[..., :ROT_DIM].astype(jnp.float32)
    t1, t2 = tf[..., :half], tf[..., half:]
    c = cos[None, :, None, :]
    sn = sin[None, :, None, :]
    rot = jnp.concatenate([t1 * c - t2 * sn, t2 * c + t1 * sn], axis=-1).astype(t.dtype)
    return jnp.concatenate([rot, t[..., ROT_DIM:]], axis=-1)

def windowed_gqa(q, k, v, sink):
    bsz, s = q.shape[:2]
    nb = s // BLOCK
    qb = q.reshape(bsz, nb, BLOCK, N_KV_HEADS, GROUP, HEAD_DIM)

    def band(t):
        tp = jnp.pad(t, ((0, 0), (BLOCK, BLOCK), (0, 0), (0, 0)))
        tp = tp.reshape(bsz, nb + 2, BLOCK, N_KV_HEADS, HEAD_DIM)
        return jnp.concatenate([tp[:, :-2], tp[:, 1:-1], tp[:, 2:]], axis=2)

    kw, vw = band(k), band(v)
    scores = jnp.einsum('bnqkgd,bnskd->bnkgqs', qb, kw).astype(jnp.float32) * (HEAD_DIM ** -0.5)
    q_idx = jnp.arange(BLOCK)[:, None]
    s_idx = jnp.arange(3 * BLOCK)[None, :]
    band_ok = jnp.abs(s_idx - BLOCK - q_idx) <= WINDOW
    key_pos = (jnp.arange(nb)[:, None] - 1) * BLOCK + jnp.arange(3 * BLOCK)[None, :]
    in_range = (key_pos >= 0) & (key_pos < s)
    mask = band_ok[None] & in_range[:, None, :]
    scores = jnp.where(mask[None, :, None, None], scores, -1e30)
    sink_l = sink.astype(jnp.float32).reshape(1, 1, N_KV_HEADS, GROUP, 1, 1)
    m = jnp.maximum(scores.max(axis=-1, keepdims=True), sink_l)
    e = jnp.exp(scores - m)
    p = e / (e.sum(axis=-1, keepdims=True) + jnp.exp(sink_l - m))
    out = jnp.einsum('bnkgqs,bnskd->bnqkgd', p.astype(v.dtype), vw)
    return out.reshape(bsz, s, ATTN_WIDTH)

def second_inputs(seed: int = 0) -> dict:
    key = jax.random.key(seed)
    ks = jax.random.split(key, 16)

    def nrm(k, shape, fan_in):
        return jax.random.normal(k, shape, jnp.float32) * (fan_in ** -0.5)

    L = DEPTH_2
    x = jax.random.normal(ks[0], (BATCH, SEQ, D_MODEL), jnp.float32)
    norm_pre_w = 1.0 + 0.02 * jax.random.normal(ks[1], (L, D_MODEL), jnp.float32)
    w_in = nrm(ks[2], (L, D_MODEL, IN_WIDTH), D_MODEL)
    conv_w = nrm(ks[3], (L, CONV_WIDTH, LRU_WIDTH), CONV_WIDTH)
    conv_b = 0.01 * jax.random.normal(ks[4], (L, LRU_WIDTH), jnp.float32)
    lru_w_r = nrm(ks[5], (L, 2, LRU_BLOCKS, LRU_BLOCK_DIM, LRU_BLOCK_DIM), LRU_BLOCK_DIM)
    lru_b_r = 0.01 * jax.random.normal(ks[6], (L, 2, LRU_WIDTH), jnp.float32)
    lru_w_i = nrm(ks[7], (L, 2, LRU_BLOCKS, LRU_BLOCK_DIM, LRU_BLOCK_DIM), LRU_BLOCK_DIM)
    lru_b_i = 0.01 * jax.random.normal(ks[8], (L, 2, LRU_WIDTH), jnp.float32)
    a_c = jax.random.uniform(ks[9], (L, 2, LRU_WIDTH), jnp.float32, minval=0.9, maxval=0.999)
    sig = a_c ** (1.0 / LRU_C)
    lru_lambda = jnp.log(sig) - jnp.log1p(-sig)
    attn_sink = jax.random.normal(ks[10], (L, N_HEADS), jnp.float32)
    w_proj_a = nrm(ks[11], (L, LRU_WIDTH, D_MODEL), LRU_WIDTH)
    w_proj_b = nrm(ks[12], (L, ATTN_WIDTH, D_MODEL), ATTN_WIDTH)
    w_out = nrm(ks[13], (L, D_MODEL, D_MODEL), D_MODEL)
    norm_post_w = 1.0 + 0.02 * jax.random.normal(ks[14], (L, D_MODEL), jnp.float32)
    return {'x': x, 'norm_pre_w': norm_pre_w, 'w_in': w_in, 'conv_w': conv_w, 'conv_b': conv_b,
            'lru_w_r': lru_w_r, 'lru_b_r': lru_b_r, 'lru_w_i': lru_w_i, 'lru_b_i': lru_b_i,
            'lru_lambda': lru_lambda, 'attn_sink': attn_sink, 'w_proj_a': w_proj_a,
            'w_proj_b': w_proj_b, 'w_out': w_out, 'norm_post_w': norm_post_w}

def second_block(x, norm_pre_w, w_in, conv_w, conv_b, lru_w_r, lru_b_r, lru_w_i, lru_b_i,
              lru_lambda, attn_sink, w_proj_a, w_proj_b, w_out, norm_post_w):
    bsz, s, _ = x.shape
    pos = jnp.arange(s, dtype=jnp.float32)
    inv_freq = ROPE_THETA ** (-jnp.arange(0, ROT_DIM, 2, dtype=jnp.float32) / ROT_DIM)
    ang = pos[:, None] * inv_freq[None, :]
    cos, sin = jnp.cos(ang), jnp.sin(ang)
    split_at = np.cumsum(IN_SPLITS)[:-1].tolist()
    for l in range(DEPTH_2):
        xn = rms_norm_2(x, norm_pre_w[l])
        z = xn @ w_in[l]
        u_lru, g_lru, q, k, v, g_attn, m_lru, m_attn = jnp.split(z, split_at, axis=-1)
        u = centred_depthwise_conv(u_lru, conv_w[l], conv_b[l])
        h = (rg_lru(u, lru_w_r[l, 0], lru_b_r[l, 0], lru_w_i[l, 0], lru_b_i[l, 0], lru_lambda[l, 0], False)
             + rg_lru(u, lru_w_r[l, 1], lru_b_r[l, 1], lru_w_i[l, 1], lru_b_i[l, 1], lru_lambda[l, 1], True))
        y_a = h.astype(x.dtype) * jax.nn.silu(g_lru)
        q = partial_rope_2(q.reshape(bsz, s, N_HEADS, HEAD_DIM), cos, sin)
        k = partial_rope_2(k.reshape(bsz, s, N_KV_HEADS, HEAD_DIM), cos, sin)
        v = v.reshape(bsz, s, N_KV_HEADS, HEAD_DIM)
        y_b = windowed_gqa(q, k, v, attn_sink[l]) * jax.nn.silu(g_attn)
        merged = (jax.nn.sigmoid(m_lru) * (y_a @ w_proj_a[l])
                  + jax.nn.sigmoid(m_attn) * (y_b @ w_proj_b[l]))
        x = x + rms_norm_2(merged @ w_out[l], norm_post_w[l])
    return x


def setup_inputs(seed=0):
    out = dict(first_inputs(seed))
    for name, value in second_inputs(seed + 1).items():
        if name != "x":
            out[name + "_2"] = value
    return out


def reference(
    x, mem, mix_norm, w_in, w_out, mem_norm, w_mem_kv, mem_q_norm, mem_k_norm, ffn_norm, w_ff1,
    w_ff2, pool_w, pool_scale, kv_norm, w_kv, k_norm, q_norm, diff_lambda, subln_norm,
    norm_pre_w_2, w_in_2, conv_w_2, conv_b_2, lru_w_r_2, lru_b_r_2, lru_w_i_2, lru_b_i_2,
    lru_lambda_2, attn_sink_2, w_proj_a_2, w_proj_b_2, w_out_2, norm_post_w_2,
):
    x = first_block(
        x, mem, mix_norm, w_in, w_out, mem_norm, w_mem_kv, mem_q_norm, mem_k_norm, ffn_norm,
        w_ff1, w_ff2, pool_w, pool_scale, kv_norm, w_kv, k_norm, q_norm, diff_lambda,
        subln_norm,
    )
    return second_block(
        x, norm_pre_w_2, w_in_2, conv_w_2, conv_b_2, lru_w_r_2, lru_b_r_2, lru_w_i_2, lru_b_i_2,
        lru_lambda_2, attn_sink_2, w_proj_a_2, w_proj_b_2, w_out_2, norm_post_w_2,
    )


_drawn_inputs = setup_inputs


def setup_inputs(seed=0):
    import zlib

    import numpy as np

    out = dict(_drawn_inputs(seed))
    spreads = {}
    factors = {'mix_norm': 5.922,
     'mem_norm': 8.0,
     'mem_q_norm': 8.0,
     'mem_k_norm': 8.0,
     'ffn_norm': 3.266,
     'kv_norm': 6.663,
     'k_norm': 8.0,
     'q_norm': 8.0,
     'subln_norm': 63.282,
     'norm_pre_w_2': 10.231,
     'conv_b_2': 16.898,
     'lru_b_r_2': 64.0,
     'lru_b_i_2': 64.0,
     'attn_sink_2': 200.0,
     'norm_post_w_2': 106.059}
    for name, (base, spread) in spreads.items():
        noise = np.random.default_rng([zlib.crc32(name.encode()), seed]).standard_normal(out[name].shape)
        drawn = base * np.exp(spread * noise) if base else spread * noise
        out[name] = __import__('jax').numpy.asarray(drawn.astype(out[name].dtype))
    for name, factor in factors.items():
        out[name] = (out[name] * factor).astype(out[name].dtype)
    return out
```

```python
import math
from contextlib import ExitStack

import numpy as np

import concourse.bass as bass
from concourse import mybir

P = 128
TOK = 256
TB = TOK // P
D = 2048
NK = D // P
GW = 512
SLAB_K = 2
NSLAB = NK // SLAB_K
SLAB = SLAB_K * GW
RAW = 4
DFF = 4 * D
NCHUNK = DFF // D
MEMW = 512
MH, MD = 4, 128
POOLW = D - MEMW
WINDOWS = (2, 4, 8, 16)
PG = POOLW // len(WINDOWS)
PGT = PG // P
DH, DK, DV = 12, 64, 128
QKW = DH * DK
LAM_INIT = 0.8 - 0.6 * math.exp(-0.3 * 1)
ROPE1 = DK // 8
H2, HD2, KVH2 = 16, 128, 4
ROPE2 = HD2 // 8
LB = 16
LRU_C = 8.0
EPS = 1e-6
THETA = 500000.0
UTW = TOK + 3

PCOL = {}
_at = 0
for _name, _n in (("mix0", NK), ("mix1", NK), ("ffn0", NK), ("ffn1", NK), ("kv", NK), ("mem0", NK),
                  ("mem1", NK), ("pre", NK), ("mq0", 1), ("mq1", 1), ("mk0", 1), ("mk1", 1), ("subln", 1),
                  ("pscale", POOLW // P), ("convw", 4 * LB), ("convb", LB), ("br", 2 * LB), ("bi", 2 * LB),
                  ("lam", 2 * LB)):
    PCOL[_name] = _at
    _at += _n
NPAR = _at
RKN, RQN, RSINK, RLAM = 0, DK, 2 * DK, 2 * DK + H2
NROW = RLAM + 4 * DK
CID, CMASK0, CCAUS, CBAND = 0, P, P + 2 * TOK, P + 4 * TOK
CR1 = P + 6 * TOK
CR2 = CR1 + 2 * TB * ROPE1
NCON = CR2 + 2 * TB * ROPE2


class N:

    def __init__(self, base, coef=0, reg=None):
        self.base, self.coef, self.reg = base, coef, reg

    def __mul__(self, k):
        return N(self.base * k, self.coef * k, self.reg)

    def __add__(self, k):
        return N(self.base + k, self.coef, self.reg)

    def half(self):
        return N(self.base // 2, self.coef // 2, self.reg)

    @property
    def v(self):
        return self.base if self.reg is None or self.coef == 0 else self.reg * self.coef + self.base


def at_least_one(n):
    return (n.base if isinstance(n, N) else n) > 0


def at(n):
    v = n.v if isinstance(n, N) else n
    assert not isinstance(v, int) or v > 0
    return v


class Group:
    def __init__(self, w, row, col, src, order=None, pieces=None):
        self.w, self.row, self.col, self.src = w, row, col, src
        self.order = order or list(range(NSLAB))
        self.pieces = pieces
        self.need = {}


class Schedule:

    def __init__(self):
        self.groups = []
        self.steps = {e: {} for e in ("pe", "act", "dve", "pool")}
        self.tails = 0
        self.staged = 0
        self.halves = 0
        self.info = {}
        self.loops = {}

    def group(self, *a, **k):
        self.groups.append(Group(*a, **k))
        return len(self.groups) - 1

    def at(self, eng, slab, name, *args):
        self.steps[eng].setdefault(slab, []).append((name, args))

    def epilogue(self, g, kind, *args, at=None):
        s = NSLAB * (g + 1) + 1 if at is None else at
        self.at("act", s, "epi_" + kind, g, *args)
        self.at("dve", s, "epi_" + kind, g, *args)

    def tail(self, slab_pe, slab_split, source, dst, kt, gain=None):
        t = self.tails
        self.tails += 1
        self.at("pe", slab_pe, "tail", t, source)
        self.at("act", slab_split, "tail", t, dst, kt, gain)
        self.at("dve", slab_split, "tail", t, dst, kt, gain)
        return t

    def attention(self, j, p, spread=1):
        for name, off in (("in", 0), ("score", 1), ("pt", 5), ("pv", 6), ("ot", 7)):
            self.at("pe", p + off * spread, "att_" + name, j)
        for name, off in (("qk", 3), ("exp", 4), ("pt", 8), ("hi", 10)):
            self.at("act", p + off * spread, "att_" + name, j)
        for name, off in (("smx", 4), ("prob", 5), ("o", 9), ("lo", 10)):
            self.at("dve", p + off * spread, "att_" + name, j)


MEMJ, DIFJ, B2J = 0, 4, 16
NJOB = B2J + H2 // 2


def plan():
    sc = Schedule()
    S = NSLAB

    for g in range(4):
        sc.tail(-9, -9, ("mem", g), 1, 4 * g, "mem0")
    g0 = sc.group("w_mem_kv0", 0, 0, 1)
    g1 = sc.group("w_mem_kv0", 0, GW, 1)
    sc.groups[g0].need[0] = [("tail_lo", sc.tails)]
    sc.epilogue(g0, "memk")
    sc.epilogue(g1, "memv")
    for g, (a, b) in enumerate(((1, 3), (5, 7), (9, 11), (13, 15))):
        sc.tail(a, b, ("x0", g), 0, 4 * g, "mix0")
    sc.at("act", 2, "x_stat", 1, -1)
    sc.at("dve", 3, "x_rstd", 1)
    q = sc.group("w_in0", 0, POOLW, 0)
    sc.groups[q].need[0] = [("tail_lo", sc.tails)]
    us = [sc.group("w_in0", 0, GW * i, 0) for i in range(3)]
    sc.epilogue(q, "store", "u", 1, POOLW)
    for i, g in enumerate(us):
        sc.epilogue(g, "store", "u", 1, GW * i)
    sc.at("dve", S * g1 + 3, "mk_norm", 0)
    sc.at("pe", S * q + 3, "mk_tp", 0)
    sc.at("act", S * q + 5, "mk_t", 0)
    sc.at("dve", S * us[0] + 2, "mq_norm", 0, q)
    sc.attention(MEMJ, S * us[0] + 4)
    sc.attention(MEMJ + 1, S * us[1] + 4)
    out0 = us[2] + 1
    for i, p in enumerate((S * us[2] + 5, S * out0, S * out0 + 2, S * out0 + 4)):
        need = us[(PG * (i + 1) - 1) // GW]
        sc.at("pool", 0, "pool_w", i)
        sc.at("pe", p, "pool_mix", i, need)
        sc.at("act", p + 1, "pool_mid", i)
        sc.at("pe", p + 1, "pool_mm", i)
        sc.at("act", p + 2, "pool_hi", i)
        sc.at("dve", p + 2, "pool_lo", i)

    def project_out(layer, first_order, need, rst_ffn):
        gs = []
        for i in range(4):
            g = sc.group(f"w_out{layer}", 0, GW * i, 1, order=first_order if i == 0 else None)
            gs.append(g)
            if i == 0:
                for s, lst in need.items():
                    sc.groups[g].need[s] = lst
            sc.epilogue(g, "add", GW * i)
            sc.at("act", S * (g + 1) + 1, "x_stat", rst_ffn, i, g)
            sc.tail(S * (g + 1) + 3, S * (g + 1) + 5, ("x", i, g), 0, 4 * i, f"ffn{layer}")
        sc.at("dve", S * (gs[3] + 1) + 2, "x_rstd", rst_ffn)

    def ffn(layer, rst, next_rst, next_dst, next_gain):
        first = sc.group(f"w_ff1{layer}", 0, 0, 0)
        sc.groups[first].need[0] = [("tail_lo", sc.tails - 1)]
        sc.groups[first].need[S - 2] = [("tail_lo", sc.tails)]
        sc.loops[first + 1] = dict(layer=layer, tail0=sc.tails, staged0=sc.staged, rst=rst)
        for _ in range(8 * (NCHUNK - 1)):
            sc.group(None, 0, 0, 0)
        sc.tails += 4 * (NCHUNK - 1)
        sc.staged += 4 * (NCHUNK - 1)
        c = NCHUNK - 1
        prev = len(sc.groups) - 1
        gs = [prev] + [sc.group(f"w_ff1{layer}", 0, D * c + GW * i, 0) for i in range(1, 4)]
        for i, g in enumerate(gs):
            sc.epilogue(g, "relu2", rst, sc.staged, sc.tails)
            sc.tail(S * (g + 1) + 3, S * (g + 1) + 5, ("staged", sc.staged), 1, 4 * i)
            sc.staged += 1
        fs = []
        for i in range(4):
            g = sc.group(f"w_ff2{layer}", D * c, GW * i, 1)
            if i == 0:
                sc.groups[g].need[0] = [("tail_lo", sc.tails - 1)]
                sc.groups[g].need[S - 2] = [("tail_lo", sc.tails)]
            sc.epilogue(g, "add", GW * i)
            sc.at("act", S * (g + 1) + 1, "x_stat", next_rst, i, g)
            fs.append(g)
        for i, g in enumerate(fs):
            sc.tail(S * (g + 1) + 3, S * (g + 1) + 5, ("x", i, g), next_dst, 4 * i, next_gain)
        sc.at("dve", S * (fs[3] + 1) + 2, "x_rstd", next_rst)

    project_out(0, [6, 7, 0, 1, 2, 3, 4, 5],
                {0: [("att_lo", MEMJ + 2)], 2: [("pool_lo", 1)], 3: [("pool_lo", 2)], 5: [("pool_lo", 3)],
                 6: [("pool_lo", 4)]}, 2)
    ffn(0, 2, 3, 0, "mix1")

    q = sc.group("w_in1", 0, POOLW, 0)
    sc.groups[q].need[0] = [("tail_lo", sc.tails - 1)]
    sc.groups[q].need[S - 2] = [("tail_lo", sc.tails)]
    us = [sc.group("w_in1", 0, GW * i, 0) for i in range(3)]
    sc.epilogue(q, "store", "u", 3, POOLW)
    for i, g in enumerate(us):
        sc.epilogue(g, "store", "u", 3, GW * i)
    sc.at("pool", S * q, "mem_again")
    for i, g in enumerate(us):
        sc.tail(S * g + 1, S * g + 3, ("mem1", i), 1, 4 * i, "mem1")
    sc.tail(S * us[2] + 5, S * us[2] + 7, ("mem1", 3), 1, 12, "mem1")
    m0 = sc.group("w_mem_kv1", 0, 0, 1)
    sc.groups[m0].need[0] = [("tail_lo", sc.tails)]
    m1 = sc.group("w_mem_kv1", 0, GW, 1)
    sc.epilogue(m0, "memk")
    sc.epilogue(m1, "memv")
    for i, s in enumerate((S * m0 + 1, S * m0 + 5, S * m1 + 1, S * m1 + 5)):
        sc.tail(s, s + 2, ("x1", i), 0, 4 * i, "kv")
    sc.at("dve", S * us[0] + 4, "mq_norm", 1, q)
    for i, g in enumerate(us):
        sc.at("dve", S * (g + 1) + 6, "q_norm", i, g)
    ks = []
    for i in range(3):
        ks.append(sc.group("w_kv", 0, 256 * i, 0, pieces=True))
        ks.append(sc.group("w_kv", 0, 2 * QKW + GW * i, 0))
    sc.groups[ks[0]].need[0] = [("tail_lo", sc.tails)]
    for i in range(3):
        sc.epilogue(ks[2 * i], "store2", 3, 256 * i)
        sc.epilogue(ks[2 * i + 1], "store", "kv", 3, 2 * QKW + GW * i, at=S * ks[5] + S - 1 if i == 2 else None)
        sc.at("dve", S * (ks[2 * i] + 1) + 2, "k_norm", i, ks[2 * i])
    sc.at("dve", S * m1 + 3, "mk_norm", 1)
    sc.at("pe", S * ks[0] + 0, "mk_tp", 1)
    sc.at("act", S * ks[0] + 2, "mk_t", 1)
    sc.attention(MEMJ + 2, S * ks[0] + 3)
    sc.attention(MEMJ + 3, S * ks[1] + 3)
    for h in range(3):
        sc.attention(DIFJ + h, S * (ks[2] + h) + 3)
    for j in range(DIFJ + 3, DIFJ + DH):
        sc.attention(j, S * ks[5] + S - 1, spread=0)
    sc.info.update(mem=(g0, m0), kv=ks)
    project_out(1, None, {0: [("att_lo", DIFJ + DH)]}, 4)
    ffn(1, 4, 5, 0, "pre")

    qs = [sc.group("w_in_2", 0, 2 * D + GW * i, 0) for i in range(4)]
    sc.groups[qs[0]].need[0] = [("tail_lo", sc.tails - 1)]
    sc.groups[qs[0]].need[S - 2] = [("tail_lo", sc.tails)]
    sc.at("pool", S * (qs[0] + 1) + 6, "x_spill", sc.tails)
    for i, g in enumerate(qs):
        sc.epilogue(g, "store", "u", 5, GW * i)
        sc.at("dve", S * (g + 1) + 3, "rope2", "u", i, g)
    k = sc.group("w_in_2", 0, 3 * D, 0)
    v = sc.group("w_in_2", 0, 3 * D + GW, 0)
    sc.epilogue(k, "store", "k2", 5, 0)
    sc.epilogue(v, "store", "v2", 5, 0)
    sc.at("dve", S * (k + 1) + 3, "rope2", "k2", 0, k)
    sc.info["k2"] = k
    ga = [sc.group("w_in_2", 0, 3 * D + 2 * GW + GW * i, 0) for i in range(4)]
    for i, g in enumerate(ga):
        sc.epilogue(g, "silu", sc.halves, sc.tails, i, 0)
        sc.at("pool", S * (g + 1) + 2, "gate_store", i, g)
        sc.halves += 1
    ul = [sc.group("w_in_2", 0, GW * i, 0) for i in range(4)]
    sc.info["ut"] = sc.tails
    for i, g in enumerate(ul):
        sc.epilogue(g, "stage", sc.tails)
        sc.tail(S * (g + 1) + 3, S * (g + 1) + 5, ("out", g), "ut", 4 * i)
    gl = [sc.group("w_in_2", 0, D + GW * i, 0) for i in range(4)]
    for i, g in enumerate(gl):
        sc.epilogue(g, "silu", sc.halves, sc.tails, 4, 0)
        sc.tail(S * (g + 1) + 3, S * (g + 1) + 5, ("out", g), "gt", 4 * i)
        sc.halves += 1
    for j in range(H2 // 2):
        sc.at("pool", S * (ga[1] + j) + 3, "gate_load", j)
        sc.attention(B2J + j, S * (ga[1] + j) + 3)
    ml = [sc.group("w_in_2", 0, 4 * D + 2 * GW + GW * i, 0) for i in range(8)]
    for i, g in enumerate(ml):
        sc.epilogue(g, "sigm", sc.halves, sc.tails, 4, i)
        sc.at("pool", S * (g + 1) + 2, "merge_store", i, g)
        sc.halves += 1
    sc.at("dve", S * ul[0] + 2, "lru_const")
    for n in range(LB):
        p = S * gl[2] + 5 * n + 4
        sc.at("pool", p - 8, "lru_w", n)
        sc.at("dve", p - 1, "conv", n)
        sc.at("pe", p, "gates", n)
        sc.at("act", p + 4, "gates", n)
        sc.at("dve", p + 5, "lru_square", n)
        sc.at("act", p + 6, "root", n)
        sc.at("dve", p + 7, "lru", n)
        sc.at("act", p + 8, "lru_hi", n)
        sc.at("dve", p + 9, "lru_lo", n)
    for i in range(4):
        a = sc.group("w_proj_a_2", 0, GW * i, 2)
        b = sc.group("w_proj_b_2", 0, GW * i, 1)
        if i == 0:
            sc.groups[a].need[0] = [("lru_lo", LB - 2)]
            sc.groups[a].need[S - 1] = [("lru_lo", LB)]
            sc.groups[b].need[0] = [("att_lo", NJOB)]
        sc.at("pool", S * a + (4 if i == 0 else 3), "merge_load", i, a)
        sc.epilogue(a, "proj_a", i)
        sc.epilogue(b, "proj_b", sc.tails)
        sc.tail(S * (b + 1) + 3, S * (b + 1) + 5, ("out", b), 0, 4 * i)
    sc.at("pool", S * (b + 1) + 1, "x_back", a)
    for i in range(4):
        g = sc.group("w_out_2", 0, GW * i, 0)
        if i == 0:
            sc.groups[g].need[0] = [("tail_lo", sc.tails - 1)]
            sc.groups[g].need[S - 2] = [("tail_lo", sc.tails)]
        sc.epilogue(g, "last", i)
    return sc


def build(nc, A, out):
    f32, f32r = mybir.dt.float32, mybir.dt.float32r
    ALU, ACT, AX = mybir.AluOpType, mybir.ActivationFunctionType, mybir.AxisListType
    sc = plan()
    S = NSLAB
    GALL = len(sc.groups)
    ctx = ExitStack()
    with ctx:
        place = {}

        def sb(name, cols, dt=f32):
            at = nc.sbuf_base
            place[name] = (at, at + 4 * cols)
            return ctx.enter_context(nc.sbuf_tensor(name, [P, cols], dt))

        def sem(name):
            return ctx.enter_context(nc.semaphore(name))

        raw = sb("raw", RAW * SLAB)
        whi, wlo = sb("whi", RAW * SLAB, f32r), sb("wlo", RAW * SLAB, f32r)
        sets = [(sb("set0_hi", NK * TOK, f32r), sb("set0_lo", NK * TOK, f32r)),
                (sb("set1_hi", NK * TOK, f32r), sb("set1_lo", NK * TOK, f32r))]
        x = sb("x", TB * D)
        u = sb("u", TB * D)
        kv = sb("kv", TB * 2 * POOLW)
        mkv = sb("mkv", 4 * GW)
        stage_a, stage_b = sb("stage_a", TB * GW), sb("stage_b", TB * GW)
        qk = sb("qk", 4 * TOK)
        prob = sb("prob", 4 * TOK)
        ob = sb("ob", 4 * P)
        scan = sb("scan", 2 * TOK)
        const, par, row = sb("const", NCON), sb("par", NPAR), sb("row", NROW)
        small = sb("small", 162)
        sets.append(tuple(nc.alloc_sbuf_tensor_at(n, [P, NK * TOK], f32r, offset=at[0])
                          for n, at in (("set2_hi", place["x"]), ("set2_lo", place["u"]))))
        poolm = kv[:, 0:8 * TOK]
        mem = kv[:, 8 * TOK:8 * TOK + TB * D]
        pw = kv[:, 8 * TOK:8 * TOK + 2 * PGT * PG]
        ut = kv[:, 0:LB * UTW]
        lw = kv[:, LB * UTW:LB * UTW + 2 * 4 * P]
        ga = kv[:, LB * UTW + 8 * P:LB * UTW + 8 * P + 4 * P]
        lb_ = kv[:, LB * UTW + 8 * P:LB * UTW + 8 * P + 2 * TOK]
        gt = x
        y = kv[:, 0:TB * D]
        gpost = u[:, 0:D]
        ident = const[:, CID:CID + P]

        SS, RS, MN = 0, 48, 60
        sumsq = [small[:, SS + 8 * k:SS + 8 * k + 8] for k in range(6)]
        rstd = [small[:, RS + 2 * k:RS + 2 * k + 2] for k in range(6)]
        half_rstd = small[:, 60:62]
        nss = small[:, 62:78]
        nrs = small[:, 78:94]
        mx, nmx = small[:, 94:98], small[:, 98:102]
        den, esink = small[:, 102:106], small[:, 106:110]
        rden = small[:, 110:114]
        lamv = small[:, 114:118]
        lsub = small[:, 118:120]
        fin_ss, fin_rs = small[:, 120:128], small[:, 128:130]
        lruc = sb("lruc", 4 * 2 * LB)
        xhs = ob

        acc = [ctx.enter_context(nc.psum_tensor(f"acc{i}", [P, TB * GW], f32)) for i in range(2)]
        tp = ctx.enter_context(nc.psum_tensor("tp", [P, 4 * TOK], f32))
        sd = ctx.enter_context(nc.psum_tensor("sd", [P, 4 * TOK], f32))

        x_dram = nc.dram_tensor("x_spill", [P, TB * D], f32, kind="Internal").ap()
        ga_dram = nc.dram_tensor("gate_spill", [P, TB * D], f32, kind="Internal").ap()
        mg_dram = nc.dram_tensor("merge_spill", [P, 8 * TB * GW], f32, kind="Internal").ap()

        ld = [sem(f"slab_loaded{i}") for i in range(RAW)]
        w_hi, w_lo, mm = sem("w_hi"), sem("w_lo"), sem("slab_multiplied")
        out_of = [sem("group_out0"), sem("group_out1")]
        names = ("tail_tp", "tail_hi", "tail_lo", "staged", "x_stat", "rstd_ok", "stage_th",
                 "att_in", "att_qk", "att_score", "att_smx", "att_exp", "att_prob", "att_pt", "att_ptc",
                 "att_pv", "att_o", "att_ot", "att_hi", "att_lo",
                 "mk_norm", "mk_tp", "mk_t", "mq_norm", "q_norm", "k_norm", "rope",
                 "pool_mix", "pool_mid", "pool_mm", "pool_hi", "pool_lo",
                 "conv_ok", "gates_pe", "gates_ok", "lru_sq", "lru_root", "lru_ok", "lru_hi", "lru_lo", "lruc_ok", "lexp_ok",
                 "lamx_ok", "lame_ok", "dve_step", "act_step", "y_ok", "ysq_ok", "fin_ok", "ut_pad",
                 "mem_in", "x_in", "con_in", "par_in", "row_in", "pm_in", "pw0_in", "pw1_in", "mem2_in",
                 "x_out", "x_again", "ga_out", "ga_in", "mg_out", "mg_in", "lw0_in", "lw1_in", "post_in",
                 "out_done", "es_ok", "sink_in")
        sm = {n: sem(n) for n in names}
        block = ctx.enter_context(nc.Block())

        W = {}
        for i in range(2):
            for n in ("w_in", "w_out", "w_mem_kv", "w_ff1", "w_ff2"):
                W[f"{n}{i}"] = A[n][i]
        W["w_kv"] = A["w_kv"]
        for n in ("w_in_2", "w_proj_a_2", "w_proj_b_2", "w_out_2"):
            W[n] = A[n][0]

        def tokens(t, lo, n, width):
            return t[:, 0:TB * width].rearrange("p (b n) -> p b n", b=TB)[:, :, lo:lo + n]

        def two(t, n=GW):
            return t[:, 0:TB * n].rearrange("p (b n) -> p b n", b=TB)

        def gout(g):
            g = g if isinstance(g, N) else N(g)
            return out_of[g.base % 2], at(g.half() + 1)

        def loads(g, s):
            per = S // RAW
            pieces = [i for i, info in enumerate(sc.groups) if info.pieces]
            more = per * len([i for i in pieces if i < g.base])
            if g.base in pieces:
                more += s // RAW + 1
            return g * per + (s // RAW + 1 + more * (SLAB_K - 1))

        def segments():
            g = 0
            while g < GALL:
                if g in sc.loops:
                    yield "loop", g, sc.loops[g]
                    g += 8 * (NCHUNK - 1)
                else:
                    yield "group", g, sc.groups[g]
                    g += 1

        def loop_groups(info, c):
            n = info["layer"]
            L = [(f"w_ff1{n}", N(0), c * D + GW * i, 0) for i in range(1, 4)]
            L += [(f"w_ff2{n}", c * D, N(GW * i), 1) for i in range(4)]
            L += [(f"w_ff1{n}", N(0), c * D + D, 0)]
            return L

        def ut_tiles(kt, n):
            return ut.rearrange("p (n t) -> p n t", t=UTW)[:, kt:kt + n, 2:2 + TOK]

        def source_ready(eng, src):
            kind = src[0]
            if kind == "mem":
                eng.wait_ge(sm["mem_in"], 16)
            elif kind == "mem1":
                eng.wait_ge(sm["mem2_in"], 16)
            elif kind == "x0":
                eng.wait_ge(sm["x_in"], 16)
            elif kind == "x":
                s, n = gout(src[2])
                eng.wait_ge(s, n)
            elif kind == "out":
                s, n = gout(src[1])
                eng.wait_ge(s, n)
            elif kind == "staged":
                eng.wait_ge(sm["staged"], at(src[1] + 1))

        def source_tile(src, j, b):
            kind = src[0]
            if kind in ("mem", "mem1"):
                return mem[:, D * b + GW * src[1] + P * j:][:, 0:P]
            if kind in ("x", "x0", "x1"):
                return x[:, D * b + GW * src[1] + P * j:][:, 0:P]
            return stage_b[:, GW * b + P * j:][:, 0:P]

        @block.sync
        def _(sp):
            def slab(g, s, w, row, col, order, pieces=None):
                n = g * S + s
                if n.base >= RAW:
                    sp.wait_ge(w_lo, at(n + (1 - RAW)))
                k = order[s] * SLAB_K * P
                rows = (row + k).v
                dst = raw[:, (s % RAW) * SLAB:(s % RAW + 1) * SLAB]
                if isinstance(rows, int):
                    src = w[rows:rows + SLAB_K * P, :]
                else:
                    src = w[bass.ds(rows, SLAB_K * P), :]
                if pieces:
                    src = src[:, 0:2 * QKW].rearrange("(t p) (m c) -> p t m c", p=P, m=2)
                    dst = dst.rearrange("p (t m c) -> p t m c", t=SLAB_K, m=2)
                    for k in range(SLAB_K):
                        sp.dma_start(dst[:, k], src[:, k, :, col.base:col.base + GW // 2])\
                            .then_inc(ld[s % RAW], 16)
                else:
                    c = col.v
                    src = src[:, c:c + GW] if isinstance(c, int) else src[:, bass.ds(c, GW)]
                    sp.dma_start(dst.rearrange("p (t n) -> p t n", t=SLAB_K),
                                 src.rearrange("(t p) n -> p t n", p=P)).then_inc(ld[s % RAW], 16)

            sp.dma_start(mem.rearrange("p (b n) -> p b n", b=TB),
                         A["mem"][0].rearrange("(b p) n -> p b n", p=P)).then_inc(sm["mem_in"], 16)
            for kind, g, info in segments():
                if kind == "group":
                    for s in range(S):
                        slab(N(g), s, W[info.w], N(info.row), N(info.col), info.order, info.pieces)
                else:
                    with sp.Fori(0, NCHUNK - 1) as c:
                        cc = N(0, 1, c)
                        for k, (w, r, col, _) in enumerate(loop_groups(info, cc)):
                            for s in range(S):
                                slab(cc * 8 + (g + k), s, W[w], r, col, list(range(S)))
            o = out[0].rearrange("(b p) n -> p b n", p=P)
            for b in range(TB):
                sp.wait_ge(sm["fin_ok"], at(b + 1))
                sp.dma_start(o[:, b], y[:, D * b:D * (b + 1)]).then_inc(sm["out_done"], 16)
            sp.wait_ge(sm["out_done"], 16 * TB)

        @block.gpsimd
        def _(pool):
            dma = nc.gpsimd.dma_start
            dma(x[:].rearrange("p (b n) -> p b n", b=TB),
                A["x"][0].rearrange("(b p) n -> p b n", p=P)).then_inc(sm["x_in"], 16)
            dma(poolm, A["poolm"]).then_inc(sm["pm_in"], 16)

            def pool_w(i):
                pool.wait_ge(sm["tail_tp"], 4)
                pool.wait_ge(sm["rstd_ok"], 1)
                if i >= 2:
                    pool.wait_ge(sm["pool_mm"], at(i - 1))
                dst = pw[:, (i % 2) * PGT * PG:(i % 2 + 1) * PGT * PG]
                dma(dst.rearrange("p (t n) -> p t n", t=PGT),
                    A["pool_w"][0, i].rearrange("(t p) n -> p t n", p=P)).then_inc(sm[f"pw{i % 2}_in"], 16)

            def mem_again():
                pool.wait_ge(sm["pool_mm"], 4)
                dma(mem.rearrange("p (b n) -> p b n", b=TB),
                    A["mem"][0].rearrange("(b p) n -> p b n", p=P)).then_inc(sm["mem2_in"], 16)

            def x_spill(tails):
                pool.wait_ge(sm["tail_tp"], at(tails))
                pool.wait_ge(sm["rstd_ok"], 6)
                dma(x_dram, x[:]).then_inc(sm["x_out"], 16)

            def gate_store(i, g):
                pool.wait_ge(*gout(g))
                dma(tokens(ga_dram, GW * i, GW, D), two(stage_b)).then_inc(sm["ga_out"], 16)

            def gate_load(j):
                pool.wait_ge(sm["ga_out"], 16 * (j // 2 + 1))
                if j:
                    pool.wait_ge(sm["att_o"], at(B2J + j))
                dma(ga.rearrange("p (b n) -> p b n", b=TB),
                    tokens(ga_dram, 2 * P * j, 2 * P, D)).then_inc(sm["ga_in"], 16)

            def merge_store(i, g):
                pool.wait_ge(*gout(g))
                dma(mg_dram[:, 2 * GW * i:2 * GW * (i + 1)], stage_b[:]).then_inc(sm["mg_out"], 16)

            def merge_load(i, a):
                pool.wait_ge(sm["mg_out"], 128)
                if i == 0:
                    pool.wait_ge(sm["att_lo"], NJOB)
                else:
                    s, n = gout(a - 1)
                    pool.wait_ge(s, n)
                dma(mkv[:, 0:2 * GW], mg_dram[:, 2 * GW * i:2 * GW * (i + 1)]).then_inc(sm["mg_in"], 16)
                dma(mkv[:, 2 * GW:4 * GW], mg_dram[:, 2 * GW * (i + 4):2 * GW * (i + 5)])\
                    .then_inc(sm["mg_in"], 16)

            def lru_w(n):
                if n >= 2:
                    pool.wait_ge(sm["gates_pe"], at(n - 1))
                dst = lw[:, (n % 2) * 4 * P:(n % 2 + 1) * 4 * P].rearrange("p (d k j) -> p d k j", d=2, k=2)
                for k, w in enumerate(("lru_w_r_2", "lru_w_i_2")):
                    dma(dst[:, :, k, :], A[w][0, :, n].rearrange("d i j -> i d j"))\
                        .then_inc(sm[f"lw{n % 2}_in"], 16)

            def x_back(a):
                pool.wait_ge(mm, at(S * (a + 1)))
                pool.wait_ge(sm["x_out"], 16)
                dma(x[:], x_dram).then_inc(sm["x_again"], 16)
                dma(gpost, A["post"]).then_inc(sm["post_in"], 16)

            steps = dict(pool_w=pool_w, mem_again=mem_again, x_spill=x_spill, gate_store=gate_store,
                         gate_load=gate_load, merge_store=merge_store, merge_load=merge_load, lru_w=lru_w,
                         x_back=x_back)
            for s in sorted(sc.steps["pool"]):
                for name, args in sc.steps["pool"][s]:
                    steps[name](*args)

        @block.scalar
        def _(act):
            A_ = nc.scalar.activation
            chain = [0]

            def link(ins):
                chain[0] += 1
                ins.then_inc(sm["act_step"], 1)
                act.wait_ge(sm["act_step"], chain[0])

            def hi(g, s):
                n = g * S + s
                act.wait_ge(ld[s % RAW], at(loads(g, s) * 16))
                if n.base >= RAW:
                    act.wait_ge(mm, at(n + (1 - RAW)))
                c = slice((s % RAW) * SLAB, (s % RAW + 1) * SLAB)
                A_(whi[:, c], raw[:, c], ACT.Copy).then_inc(w_hi, 1)

            def acc_of(g):
                g = g if isinstance(g, N) else N(g)
                act.wait_ge(mm, at(g * S + S))
                return acc[g.base % 2], out_of[g.base % 2]

            def scaled(g, k, dst):
                act.wait_ge(sm["rstd_ok"], at(k + 1))
                a, done = acc_of(g)
                for b in range(TB):
                    ins = A_(dst[b], a[:, GW * b:GW * (b + 1)], ACT.Copy, scale=rstd[k][:, b:b + 1])
                ins.then_inc(done, 1)

            def epi_memk(g):
                scaled(g, 0, [prob[:, 0:GW], prob[:, GW:2 * GW]])

            def epi_memv(g):
                scaled(g, 0, [mkv[:, 2 * GW:3 * GW], mkv[:, 3 * GW:4 * GW]])

            def epi_store(g, where, k, col):
                if where == "u":
                    dst = [u[:, D * b + col:D * b + col + GW] for b in range(TB)]
                elif where == "kv":
                    dst = [kv[:, 2 * POOLW * b + col:2 * POOLW * b + col + GW] for b in range(TB)]
                else:
                    o = 0 if where == "k2" else TB * GW
                    dst = [mkv[:, o + GW * b:o + GW * (b + 1)] for b in range(TB)]
                scaled(g, k, dst)

            def epi_store2(g, k, col):
                act.wait_ge(sm["rstd_ok"], at(k + 1))
                a, done = acc_of(g)
                for b in range(TB):
                    dst = kv[:, 2 * POOLW * b:2 * POOLW * b + 2 * QKW]
                    dst = dst.rearrange("p (m c) -> p m c", m=2)[:, :, col:col + GW // 2]
                    ins = A_(dst, a[:, GW * b:GW * (b + 1)].rearrange("p (m c) -> p m c", m=2), ACT.Copy,
                             scale=rstd[k][:, b:b + 1])
                ins.then_inc(done, 1)

            def epi_relu2(g, k, q, tails=None):
                act.wait_ge(sm["rstd_ok"], at(k + 1))
                if at_least_one(q):
                    act.wait_ge(sm["staged"], at(q))
                a, done = acc_of(g)
                for b in range(TB):
                    ins = A_(stage_a[:, GW * b:GW * (b + 1)], a[:, GW * b:GW * (b + 1)], ACT.Relu,
                             scale=rstd[k][:, b:b + 1])
                ins.then_inc(done, 1)

            def epi_stage(g, tails):
                act.wait_ge(sm["tail_tp"], at(tails))
                act.wait_ge(sm["ga_out"], 64)
                scaled(g, 5, [stage_b[:, GW * b:GW * (b + 1)] for b in range(TB)])

            def epi_tanh(g, n, tails, stored, merged):
                act.wait_ge(sm["rstd_ok"], 6)
                act.wait_ge(*gout(g - 1))
                a, _ = acc_of(g)
                for b in range(TB):
                    ins = A_(stage_a[:, GW * b:GW * (b + 1)], a[:, GW * b:GW * (b + 1)], ACT.Tanh,
                             scale=half_rstd[:, b:b + 1])
                ins.then_inc(sm["stage_th"], 1)

            def epi_last(g, i):
                a, done = acc_of(g)
                for b in range(TB):
                    A_(y[:, D * b + GW * i:D * b + GW * (i + 1)], a[:, GW * b:GW * (b + 1)], ACT.Copy)
                for b in range(TB):
                    ins = A_(qk[:, GW * b:GW * (b + 1)], a[:, GW * b:GW * (b + 1)], ACT.Square,
                             accum_out=fin_ss[:, 4 * b + i:4 * b + i + 1])
                ins.then_inc(done, 1)

            def x_stat(k, i, g=None):
                if i < 0:
                    act.wait_ge(sm["x_in"], 16)
                    for b in range(TB):
                        for i in range(4):
                            ins = A_(qk[:, 0:GW], x[:, D * b + GW * i:D * b + GW * (i + 1)], ACT.Square,
                                     accum_out=sumsq[k][:, 4 * b + i:4 * b + i + 1])
                            link(ins)
                    A_(lsub[:, 0:1], sumsq[k][:, 0:1], ACT.Copy).then_inc(sm["x_stat"], 4)
                    return
                s, n = gout(g)
                act.wait_ge(s, n)
                for b in range(TB):
                    ins = A_(qk[:, GW * b:GW * (b + 1)], x[:, D * b + GW * i:D * b + GW * (i + 1)],
                             ACT.Square, accum_out=sumsq[k][:, 4 * b + i:4 * b + i + 1])
                ins.then_inc(sm["x_stat"], 1)

            def tail(t, dst, kt, gain):
                t = t if isinstance(t, N) else N(t)
                act.wait_ge(sm["tail_tp"], at(t + 1))
                if dst == "ut":
                    ins = A_(ut_tiles(kt, 2), tp[:, 0:2 * TOK].rearrange("p (n t) -> p n t", n=2), ACT.Copy)
                elif dst == "gt":
                    act.wait_ge(sm["x_out"], 16)
                    ins = A_(gt[:, TOK * kt:TOK * (kt + 2)], tp[:, 0:2 * TOK], ACT.Copy)
                elif gain is None:
                    ins = A_(sets[dst][0][:, TOK * kt:TOK * (kt + 4)], tp[:], ACT.Copy)
                else:
                    for j in range(4):
                        c = PCOL[gain] + kt + j
                        ins = A_(sets[dst][0][:, TOK * (kt + j):TOK * (kt + j + 1)],
                                 tp[:, TOK * j:TOK * (j + 1)], ACT.Copy, scale=par[:, c:c + 1])
                ins.then_inc(sm["tail_hi"], 1)

            def mk_t(l):
                act.wait_ge(sm["mk_tp"], at(l + 1))
                A_(mkv[:, 0:4 * TOK], sd[:], ACT.Copy,
                   scale=par[:, PCOL[f"mk{l}"]:PCOL[f"mk{l}"] + 1]).then_inc(sm["mk_t"], 1)

            def att_qk(j):
                act.wait_ge(sm["att_in"], at(j + 1))
                if j < DIFJ:
                    c = PCOL[f"mq{j // 2}"]
                    ins = A_(qk[:, 0:2 * TOK], sd[:, 0:2 * TOK], ACT.Copy, scale=par[:, c:c + 1])
                elif j < B2J:
                    ins = A_(qk[0:DK, :], sd[0:DK, :], ACT.Copy)
                else:
                    ins = A_(qk[:, 0:3 * TOK], sd[:, 0:3 * TOK], ACT.Copy)
                ins.then_inc(sm["att_qk"], 1)

            def att_exp(j):
                act.wait_ge(sm["att_smx"], at(j + 1))
                if j >= B2J:
                    A_(esink, esink, ACT.Exp)
                for r in range(4):
                    ins = A_(prob[:, TOK * r:TOK * (r + 1)], prob[:, TOK * r:TOK * (r + 1)], ACT.Exp,
                             bias=nmx[:, r:r + 1], accum_out=den[:, r:r + 1])
                ins.then_inc(sm["att_exp"], 1)

            def att_pt(j):
                act.wait_ge(sm["att_pt"], at(j + 1))
                n = 2 * TOK if DIFJ <= j < B2J else 4 * TOK
                A_(qk[:, 0:n], sd[:, 0:n], ACT.Copy).then_inc(sm["att_ptc"], 1)

            def att_dst(j):
                if j < DIFJ:
                    return NK - MH + 2 * (j % 2), 2 * TOK
                return (j - DIFJ, TOK) if j < B2J else (2 * (j - B2J), 2 * TOK)

            def att_hi(j):
                act.wait_ge(sm["att_ot"], at(j + 1))
                kt, n = att_dst(j)
                dst = sets[1][0][:, TOK * kt:TOK * kt + n]
                if DIFJ <= j < B2J:
                    ins = A_(dst, sd[:, 0:n], ACT.Copy, scale=lsub[:, 1:2])
                else:
                    ins = A_(dst, sd[:, 0:n], ACT.Copy)
                ins.then_inc(sm["att_hi"], 1)

            def pool_mid(i):
                act.wait_ge(sm["pool_mix"], at(i + 1))
                A_(qk[:, 0:PGT * TOK], sd[:, 0:PGT * TOK], ACT.Copy).then_inc(sm["pool_mid"], 1)

            def pool_hi(i):
                act.wait_ge(sm["pool_mm"], at(i + 1))
                for t in range(PGT):
                    kt = PGT * i + t
                    c = PCOL["pscale"] + kt
                    ins = A_(sets[1][0][:, TOK * kt:TOK * (kt + 1)], sd[:, TOK * t:TOK * (t + 1)], ACT.Copy,
                             scale=par[:, c:c + 1])
                ins.then_inc(sm["pool_hi"], 1)

            def gates(n):
                act.wait_ge(sm["gates_pe"], at(n + 1))
                act.wait_ge(sm["lruc_ok"], 1)
                if n:
                    act.wait_ge(sm["lru_ok"], at(n))
                for d in range(2):
                    for k in range(2):
                        c = (2 + k) * 2 * LB + LB * d + n
                        o = (2 * k + d) * TOK
                        ins = A_(prob[:, o:o + TOK], sd[:, (2 * d + k) * TOK:(2 * d + k + 1) * TOK],
                                 ACT.Tanh, bias=lruc[:, c:c + 1], scale=0.5)
                link(ins)
                for d in range(2):
                    th = prob[:, d * TOK:(d + 1) * TOK]
                    c, m = LB * d + n, 2 * LB + LB * d + n
                    A_(qk[:, d * TOK:(d + 1) * TOK], th, ACT.Exp,
                       bias=lruc[:, m:m + 1], scale=lruc[:, m:m + 1])
                    ins = A_(qk[:, (2 + d) * TOK:(3 + d) * TOK], th, ACT.Tanh,
                             bias=lruc[:, c:c + 1], scale=lruc[:, c:c + 1])
                ins.then_inc(sm["gates_ok"], 1)

            def root(n):
                act.wait_ge(sm["lru_sq"], n + 1)
                A_(lb_, lb_, ACT.Sqrt, scale=0.25).then_inc(sm["lru_root"], 1)

            def lru_hi(n):
                act.wait_ge(sm["lru_ok"], at(n + 1))
                A_(sets[2][0][:, TOK * n:TOK * (n + 1)], scan[:, 0:TOK], ACT.Copy).then_inc(sm["lru_hi"], 1)

            steps = dict(epi_memk=epi_memk, epi_memv=epi_memv, epi_store=epi_store, epi_store2=epi_store2,
                         epi_relu2=epi_relu2, epi_stage=epi_stage, epi_silu=epi_tanh, epi_sigm=epi_tanh,
                         epi_last=epi_last, x_stat=x_stat, tail=tail, mk_t=mk_t, att_qk=att_qk,
                         att_exp=att_exp, att_pt=att_pt, att_hi=att_hi, pool_mid=pool_mid, pool_hi=pool_hi,
                         gates=gates, root=root, lru_hi=lru_hi, epi_add=None, epi_proj_a=None, epi_proj_b=None)

            def run(slab):
                for name, args in sc.steps["act"].get(slab, ()):
                    if steps[name]:
                        steps[name](*args)

            act.dma_start(const[:], A["const"]).then_inc(sm["con_in"], 16)
            act.dma_start(par[:], A["par"]).then_inc(sm["par_in"], 16)
            act.dma_start(row[:], A["row"]).then_inc(sm["row_in"], 16)
            act.wait_ge(sm["mem_in"], 16)
            for b in range(TB):
                for i in range(4):
                    ins = A_(qk[:, 0:GW], mem[:, D * b + GW * i:D * b + GW * (i + 1)], ACT.Square,
                             accum_out=sumsq[0][:, 4 * b + i:4 * b + i + 1])
                    link(ins)
            A_(lsub[:, 0:1], sumsq[0][:, 0:1], ACT.Copy).then_inc(sm["x_stat"], 4)
            act.wait_ge(sm["par_in"], 16)
            act.wait_ge(sm["lamx_ok"], 1)
            A_(lamv[:, 2:4], lamv[:, 0:2], ACT.Exp).then_inc(sm["lame_ok"], 1)
            A_(lruc[:, 6 * LB:8 * LB], lruc[:, 0:2 * LB], ACT.Exp, scale=-1.0).then_inc(sm["lexp_ok"], 1)
            run(-9)
            for kind, g, info in segments():
                if kind == "group":
                    for s in range(S):
                        hi(N(g), s)
                        run(S * g + s)
                else:
                    with act.Fori(0, NCHUNK - 1) as c:
                        cc = N(0, 1, c)
                        for k in range(8):
                            for s in range(S):
                                hi(cc * 8 + (g + k), s)
                                q = cc * 4 + (info["staged0"] + k)
                                t = cc * 4 + (info["tail0"] + k)
                                if s == 1 and k < 4:
                                    epi_relu2(cc * 8 + (g + k - 1), info["rst"], q, t)
                                if s == 5 and k < 4:
                                    tail(t, 1, 4 * k, None)
            run(S * GALL + 1)

        @block.vector
        def _(dve):
            V = nc.vector
            chain = [0]

            def link(ins):
                chain[0] += 1
                ins.then_inc(sm["dve_step"], 1)
                dve.wait_ge(sm["dve_step"], chain[0])

            def lo(g, s):
                dve.wait_ge(w_hi, at(g * S + (s + 1)))
                c = slice((s % RAW) * SLAB, (s % RAW + 1) * SLAB)
                V.tensor_tensor(wlo[:, c], raw[:, c], whi[:, c].bitcast(f32), ALU.subtract).then_inc(w_lo, 1)

            def acc_of(g):
                g = g if isinstance(g, N) else N(g)
                dve.wait_ge(mm, at(g * S + S))
                return acc[g.base % 2], out_of[g.base % 2]

            def rms(dst, ssq, n, count):
                v, h = small[:, 130:130 + count], small[:, 146:146 + count]
                i32 = mybir.dt.int32
                link(V.tensor_scalar(v, ssq, 1.0 / n, EPS, ALU.mult, ALU.add))
                link(V.tensor_scalar(h.bitcast(i32), v.bitcast(i32), 1, None, ALU.logical_shift_right))
                link(V.tensor_scalar(dst.bitcast(i32), h.bitcast(i32), -1.0, float(0x5F3759DF), ALU.mult,
                                     ALU.add))
                for k in range(4):
                    link(V.tensor_tensor(h, dst, dst, ALU.mult))
                    link(V.tensor_tensor(h, h, v, ALU.mult))
                    link(V.tensor_scalar(h, h, -0.5, 1.5, ALU.mult, ALU.add))
                    ins = V.tensor_tensor(dst, dst, h, ALU.mult)
                    if k < 3:
                        link(ins)
                return ins

            def epi_add(g, col):
                a, done = acc_of(g)
                xs = tokens(x, col, GW, D)
                V.tensor_tensor(xs, two(a), xs, ALU.add).then_inc(done, 1)

            def epi_relu2(g, k, q, tails):
                dve.wait_ge(*gout(g))
                dve.wait_ge(sm["tail_tp"], at(tails))
                V.tensor_tensor(stage_b[:], stage_a[:], stage_a[:], ALU.mult).then_inc(sm["staged"], 1)

            def stage_b_free(tails, stored, merged):
                dve.wait_ge(sm["tail_tp"], at(tails))
                if stored:
                    dve.wait_ge(sm["ga_out"], at(16 * stored))
                if merged:
                    dve.wait_ge(sm["mg_out"], at(16 * merged))

            def epi_silu(g, n, tails, stored, merged):
                dve.wait_ge(sm["stage_th"], at(n + 1))
                stage_b_free(tails, stored, merged)
                a, done = acc_of(g)
                link(V.tensor_scalar(stage_a[:], stage_a[:], 1.0, None, ALU.add))
                for b in range(TB):
                    c = slice(GW * b, GW * (b + 1))
                    ins = V.scalar_tensor_tensor(out=stage_b[:, c], in0=a[:, c], scalar=half_rstd[:, b:b + 1],
                                                 in1=stage_a[:, c], op0=ALU.mult, op1=ALU.mult)
                ins.then_inc(done, 1)

            def epi_sigm(g, n, tails, stored, merged):
                dve.wait_ge(sm["stage_th"], at(n + 1))
                stage_b_free(tails, stored, merged)
                V.tensor_scalar(stage_b[:], stage_a[:], 0.5, 0.5, ALU.mult, ALU.add).then_inc(out_of[g % 2], 1)

            def epi_proj_a(g, i):
                dve.wait_ge(sm["mg_in"], at(32 * (i + 1)))
                a, done = acc_of(g)
                V.tensor_tensor(stage_a[:], a[:], mkv[:, 0:2 * GW], ALU.mult).then_inc(done, 1)

            def epi_proj_b(g, tails):
                a, done = acc_of(g)
                stage_b_free(tails, 4, 8)
                link(V.tensor_tensor(stage_b[:], a[:], mkv[:, 2 * GW:4 * GW], ALU.mult))
                V.tensor_tensor(stage_b[:], stage_b[:], stage_a[:], ALU.add).then_inc(done, 1)

            def x_rstd(k):
                dve.wait_ge(sm["x_stat"], at(4 * (k + 1)))
                link(V.tensor_reduce(rstd[k], sumsq[k].rearrange("p (b n) -> p b n", b=TB), AX.X, ALU.add))
                if k == 5:
                    link(rms(rstd[k], rstd[k], D, TB))
                    V.tensor_scalar(half_rstd, rstd[k], 0.5, None, ALU.mult).then_inc(sm["rstd_ok"], 1)
                else:
                    rms(rstd[k], rstd[k], D, TB).then_inc(sm["rstd_ok"], 1)

            def tail(t, dst, kt, gain):
                t = t if isinstance(t, N) else N(t)
                dve.wait_ge(sm["tail_hi"], at(t + 1))
                if dst == "ut":
                    V.tensor_copy(ut_tiles(kt + 2, 2), tp[:, 2 * TOK:4 * TOK].rearrange("p (n t) -> p n t", n=2))\
                        .then_inc(sm["tail_lo"], 1)
                    return
                if dst == "gt":
                    V.tensor_copy(gt[:, TOK * (kt + 2):TOK * (kt + 4)], tp[:, 2 * TOK:4 * TOK])\
                        .then_inc(sm["tail_lo"], 1)
                    return
                h, l = sets[dst]
                if gain is None:
                    c = slice(TOK * kt, TOK * (kt + 4))
                    ins = V.tensor_tensor(l[:, c], tp[:], h[:, c].bitcast(f32), ALU.subtract)
                else:
                    for j in range(4):
                        p = PCOL[gain] + kt + j
                        c = slice(TOK * (kt + j), TOK * (kt + j + 1))
                        ins = V.scalar_tensor_tensor(out=l[:, c], in0=tp[:, TOK * j:TOK * (j + 1)],
                                                     scalar=par[:, p:p + 1], in1=h[:, c].bitcast(f32),
                                                     op0=ALU.mult, op1=ALU.subtract)
                ins.then_inc(sm["tail_lo"], 1)

            def head_norm(t, n, d, tmp):
                link(V.tensor_tensor(tmp, t, t, ALU.mult))
                ss, rs = nss[:, 0:n], nrs[:, 0:n]
                if len(t.shape) == 4:
                    ss4 = ss.rearrange("p (b h) -> p b h", b=TB)
                    rs4 = rs.rearrange("p (b h) -> p b h", b=TB)
                else:
                    ss4, rs4 = ss, rs
                link(V.tensor_reduce(ss4, tmp, AX.X, ALU.add))
                link(rms(rs, ss, d, n))
                return V.tensor_tensor(t, t, rs4.unsqueeze(len(t.shape) - 1).broadcast_to(list(t.shape)), ALU.mult)

            def mk_norm(l):
                s, n = gout(sc.info["mem"][l])
                dve.wait_ge(s, n)
                t = prob[:].rearrange("p (n d) -> p n d", d=MD)
                head_norm(t, 2 * MH, MD, stage_a[:].rearrange("p (n d) -> p n d", d=MD)).then_inc(sm["mk_norm"], 1)

            def mq_norm(l, g):
                s, n = gout(g)
                dve.wait_ge(s, n)
                t = tokens(u, POOLW, MEMW, D).rearrange("p b (h d) -> p b h d", d=MD)
                tmp = stage_a[:].rearrange("p (b h d) -> p b h d", b=TB, d=MD)
                head_norm(t, 2 * MH, MD, tmp).then_inc(sm["mq_norm"], 1)

            def rope(t, heads, half, ccol, out_sem):
                cs = const[:, ccol:ccol + 2 * TB * half].rearrange("p (k b n) -> p k b n", k=2, b=TB)
                n = TB * heads * half
                tmp = [stage_a[:, n * i:n * (i + 1)].rearrange("p (b h d) -> p b h d", b=TB, h=heads)
                       for i in range(4)]
                t1, t2 = t[:, :, :, 0:half], t[:, :, :, half:2 * half]
                for b in range(TB):
                    c_ = cs[:, 0, b, :].unsqueeze(1).broadcast_to([P, heads, half])
                    s_ = cs[:, 1, b, :].unsqueeze(1).broadcast_to([P, heads, half])
                    V.tensor_tensor(tmp[0][:, b], t1[:, b], c_, ALU.mult)
                    V.tensor_tensor(tmp[1][:, b], t2[:, b], s_, ALU.mult)
                    V.tensor_tensor(tmp[2][:, b], t1[:, b], s_, ALU.mult)
                    ins = V.tensor_tensor(tmp[3][:, b], t2[:, b], c_, ALU.mult)
                link(ins)
                V.tensor_tensor(t1, tmp[0], tmp[1], ALU.subtract)
                V.tensor_tensor(t2, tmp[2], tmp[3], ALU.add).then_inc(out_sem, 1)

            def diff_norm(t, gcol, out_sem):
                tmp = stage_a[:].rearrange("p (b h d) -> p b h d", b=TB, d=DK)
                link(head_norm(t, 16, DK, tmp))
                for b in range(TB):
                    gb = row[:, gcol:gcol + DK].unsqueeze(1).broadcast_to([P, 8, DK])
                    ins = V.tensor_tensor(t[:, b], t[:, b], gb, ALU.mult)
                link(ins)
                rope(t, 8, ROPE1, CR1, out_sem)

            def q_norm(i, g):
                s, n = gout(g)
                dve.wait_ge(s, n)
                diff_norm(tokens(u, GW * i, GW, D).rearrange("p b (h d) -> p b h d", d=DK), RQN, sm["q_norm"])

            def k_norm(i, g):
                s, n = gout(g)
                dve.wait_ge(s, n)
                for m in range(2):
                    t = tokens(kv, QKW * m + 256 * i, 256, 2 * POOLW).rearrange("p b (h d) -> p b h d", d=DK)
                    tmp = stage_a[:, 0:TB * 256].rearrange("p (b h d) -> p b h d", b=TB, d=DK)
                    link(head_norm(t, 8, DK, tmp))
                    for b in range(TB):
                        gb = row[:, RKN:RKN + DK].unsqueeze(1).broadcast_to([P, 4, DK])
                        ins = V.tensor_tensor(t[:, b], t[:, b], gb, ALU.mult)
                    link(ins)
                    rope(t, 4, ROPE1, CR1, sm["k_norm"])
                    dve.wait_ge(sm["k_norm"], 2 * i + m + 1)

            def rope2(where, i, g):
                s, n = gout(g)
                dve.wait_ge(s, n)
                if where == "u":
                    t = tokens(u, GW * i, GW, D)
                else:
                    t = two(mkv)
                rope(t.rearrange("p b (h d) -> p b h d", d=HD2), 4, ROPE2, CR2, sm["rope"])

            def att_smx(j):
                dve.wait_ge(sm["att_score"], at(j + 1))
                if j:
                    dve.wait_ge(sm["att_pt"], at(j))
                m, scale = (CMASK0, MD ** -0.5) if j < DIFJ else (CCAUS, DK ** -0.5) if j < B2J \
                    else (CBAND, HD2 ** -0.5)
                pr = prob[:].rearrange("p (r n) -> p r n", r=2)
                ps = sd[:].rearrange("p (r n) -> p r n", r=2)
                mk = const[:, m:m + 2 * TOK]
                for r in range(2):
                    ins = V.scalar_tensor_tensor(out=pr[:, r], in0=ps[:, r], scalar=scale, in1=mk,
                                                 op0=ALU.mult, op1=ALU.add)
                link(ins)
                link(V.tensor_reduce(mx, prob[:].rearrange("p (r n) -> p r n", r=4), AX.X, ALU.max))
                if j >= B2J:
                    sk = row[:, RSINK + 2 * (j - B2J):RSINK + 2 * (j - B2J) + 2]
                    sk = sk.unsqueeze(2).broadcast_to([P, 2, TB])
                    link(V.tensor_tensor(mx.rearrange("p (h b) -> p h b", b=TB),
                                         mx.rearrange("p (h b) -> p h b", b=TB), sk, ALU.max))
                    link(V.tensor_tensor(esink.rearrange("p (h b) -> p h b", b=TB), sk,
                                         mx.rearrange("p (h b) -> p h b", b=TB), ALU.subtract))
                V.tensor_scalar(nmx, mx, -1.0, None, ALU.mult).then_inc(sm["att_smx"], 1)

            def att_prob(j):
                dve.wait_ge(sm["att_exp"], at(j + 1))
                if j >= B2J:
                    link(V.tensor_tensor(den, den, esink, ALU.add))
                if not DIFJ <= j < B2J:
                    V.reciprocal(rden, den).then_inc(sm["att_prob"], 1)
                    return
                link(V.reciprocal(rden, den))
                link(V.tensor_scalar(rden[:, 2:4], rden[:, 2:4], lamv[:, 2:3], None, ALU.mult))
                for b in range(TB):
                    c2 = slice(TOK * (2 + b), TOK * (3 + b))
                    ins = V.tensor_scalar(prob[:, c2], prob[:, c2], rden[:, 2 + b:3 + b], None, ALU.mult)
                link(ins)
                for b in range(TB):
                    c1, c2 = slice(TOK * b, TOK * (b + 1)), slice(TOK * (2 + b), TOK * (3 + b))
                    ins = V.scalar_tensor_tensor(out=prob[:, c1], in0=prob[:, c1], scalar=rden[:, b:b + 1],
                                                 in1=prob[:, c2], op0=ALU.mult, op1=ALU.add)
                ins.then_inc(sm["att_prob"], 1)

            def att_o(j):
                dve.wait_ge(sm["att_pv"], at(j + 1))
                if j:
                    dve.wait_ge(sm["att_ot"], at(j))
                if DIFJ <= j < B2J:
                    link(V.tensor_copy(ob[:, 0:2 * P], sd[:, 0:2 * P]))
                    t = ob[:, 0:2 * P].rearrange("p (b d) -> p b d", b=TB)
                    tmp = ob[:, 2 * P:4 * P].rearrange("p (b d) -> p b d", b=TB)
                    head_norm(t, TB, DV, tmp).then_inc(sm["att_o"], 1)
                    return
                r = rden.unsqueeze(2).broadcast_to([P, 4, P])
                o4 = ob[:].rearrange("p (r d) -> p r d", r=4)
                ins = V.tensor_tensor(o4, sd[:, 0:4 * P].rearrange("p (r d) -> p r d", r=4), r, ALU.mult)
                if j >= B2J:
                    link(ins)
                    dve.wait_ge(sm["ga_in"], at(16 * (j - B2J + 1)))
                    g4 = ga.rearrange("p (b h d) -> p b h d", b=TB, h=2)
                    for h in range(2):
                        oo = ob[:, 2 * P * h:2 * P * (h + 1)].rearrange("p (b d) -> p b d", b=TB)
                        ins = V.tensor_tensor(oo, oo, g4[:, :, h, :], ALU.mult)
                ins.then_inc(sm["att_o"], 1)

            def att_lo(j):
                dve.wait_ge(sm["att_hi"], at(j + 1))
                if j < DIFJ:
                    kt, n = NK - MH + 2 * (j % 2), 2 * TOK
                elif j < B2J:
                    kt, n = j - DIFJ, TOK
                else:
                    kt, n = 2 * (j - B2J), 2 * TOK
                c = slice(TOK * kt, TOK * kt + n)
                h, l = sets[1]
                if DIFJ <= j < B2J:
                    ins = V.scalar_tensor_tensor(out=l[:, c], in0=sd[:, 0:n], scalar=lsub[:, 1:2],
                                                 in1=h[:, c].bitcast(f32), op0=ALU.mult, op1=ALU.subtract)
                else:
                    ins = V.tensor_tensor(l[:, c], sd[:, 0:n], h[:, c].bitcast(f32), ALU.subtract)
                ins.then_inc(sm["att_lo"], 1)

            def pool_lo(i):
                dve.wait_ge(sm["pool_hi"], at(i + 1))
                h, l = sets[1]
                for t in range(PGT):
                    kt = PGT * i + t
                    c = slice(TOK * kt, TOK * (kt + 1))
                    p = PCOL["pscale"] + kt
                    ins = V.scalar_tensor_tensor(out=l[:, c], in0=sd[:, TOK * t:TOK * (t + 1)],
                                                 scalar=par[:, p:p + 1], in1=h[:, c].bitcast(f32),
                                                 op0=ALU.mult, op1=ALU.subtract)
                ins.then_inc(sm["pool_lo"], 1)

            def lru_const():
                pad = ut.rearrange("p (n t) -> p n t", t=UTW)
                V.memset(pad[:, :, 0:2], 0.0)
                V.memset(pad[:, :, UTW - 1:UTW], 0.0).then_inc(sm["ut_pad"], 1)

            def conv(n):
                dve.wait_ge(sm["tail_hi"], at(sc.info["ut"] + n // 4 + 1))
                dve.wait_ge(sm["tail_lo"], sc.info["ut"] + n // 4 + 1)
                dve.wait_ge(sm["ut_pad"], 1)
                if n >= 2:
                    dve.wait_ge(sm["gates_pe"], at(n - 1))
                dve.wait_ge(sm["att_ot"], NJOB)
                xh = xhs[:, TOK * (n % 2):TOK * (n % 2 + 1)]
                base = UTW * n
                pc = PCOL["convw"] + 4 * n
                link(V.tensor_scalar(xh, ut[:, base:base + TOK], par[:, pc:pc + 1],
                                     par[:, PCOL["convb"] + n:PCOL["convb"] + n + 1], ALU.mult, ALU.add))
                for k in range(1, 4):
                    ins = V.scalar_tensor_tensor(out=xh, in0=ut[:, base + k:base + k + TOK],
                                                 scalar=par[:, pc + k:pc + k + 1], in1=xh,
                                                 op0=ALU.mult, op1=ALU.add)
                    if k < 3:
                        link(ins)
                ins.then_inc(sm["conv_ok"], 1)

            def lru_square(n):
                dve.wait_ge(sm["gates_ok"], at(n + 1))
                if n:
                    dve.wait_ge(sm["lru_lo"], at(n))
                dve.wait_ge(sm["att_o"], NJOB)
                xh = xhs[:, TOK * (n % 2):TOK * (n % 2 + 1)]
                Tt = qk[:, 2 * TOK:4 * TOK]
                link(V.tensor_tensor(scan[:], qk[:, 0:2 * TOK], qk[:, 0:2 * TOK], ALU.mult))
                for d in range(2):
                    c = slice((2 + d) * TOK, (3 + d) * TOK)
                    ins = V.scalar_tensor_tensor(out=prob[:, c], in0=prob[:, c], scalar=1.0, in1=xh,
                                                 op0=ALU.add, op1=ALU.mult)
                V.scalar_tensor_tensor(out=lb_, in0=scan[:], scalar=1.0, in1=Tt, op0=ALU.add,
                                       op1=ALU.mult).then_inc(sm["lru_sq"], 1)

            def lru(n):
                dve.wait_ge(sm["lru_root"], n + 1)
                link(V.tensor_tensor(lb_, lb_, prob[:, 2 * TOK:4 * TOK], ALU.mult))
                V.tensor_tensor_scan(scan[:, 0:TOK], qk[:, 0:TOK], lb_[:, 0:TOK], 0.0, ALU.mult, ALU.add)
                link(V.tensor_tensor_scan(scan[:, TOK:2 * TOK][:, ::-1], qk[:, TOK:2 * TOK][:, ::-1],
                                          lb_[:, TOK:2 * TOK][:, ::-1], 0.0, ALU.mult, ALU.add))
                link(V.tensor_tensor(scan[:, 0:TOK], scan[:, 0:TOK], scan[:, TOK:2 * TOK], ALU.add))
                V.tensor_tensor(scan[:, 0:TOK], scan[:, 0:TOK], gt[:, TOK * n:TOK * (n + 1)], ALU.mult)\
                    .then_inc(sm["lru_ok"], 1)

            def lru_lo(n):
                dve.wait_ge(sm["lru_hi"], at(n + 1))
                h, l = sets[2]
                c = slice(TOK * n, TOK * (n + 1))
                V.tensor_tensor(l[:, c], scan[:, 0:TOK], h[:, c].bitcast(f32), ALU.subtract)\
                    .then_inc(sm["lru_lo"], 1)

            def start():
                dve.wait_ge(sm["row_in"], 16)
                dve.wait_ge(sm["par_in"], 16)
                for i in range(2):
                    a = row[:, RLAM + 2 * DK * i:RLAM + 2 * DK * i + DK]
                    b = row[:, RLAM + 2 * DK * i + DK:RLAM + 2 * DK * (i + 1)]
                    ins = V.tensor_tensor(ob[:, DK * i:DK * (i + 1)], a, b, ALU.mult)
                link(ins)
                V.tensor_reduce(lamv[:, 0:2], ob[:, 0:2 * DK].rearrange("p (n d) -> p n d", d=DK), AX.X, ALU.add)
                lam = par[:, PCOL["lam"]:PCOL["lam"] + 2 * LB]
                w = 2 * LB
                link(V.tensor_scalar(lsub[:, 1:2], par[:, PCOL["subln"]:PCOL["subln"] + 1],
                                     1.0 - LAM_INIT, None, ALU.mult))
                link(V.tensor_scalar(lruc[:, 0:w], lam, -1.0, None, ALU.mult))
                V.tensor_tensor(lruc[:, 0:w], lruc[:, 0:w], lam, ALU.max).then_inc(sm["lamx_ok"], 1)
                dve.wait_ge(sm["lame_ok"], 1)
                link(V.tensor_tensor(lamv[:, 2:3], lamv[:, 3:4], lamv[:, 2:3], ALU.subtract))
                link(V.tensor_scalar(lamv[:, 2:3], lamv[:, 2:3], -LAM_INIT, None, ALU.add))
                dve.wait_ge(sm["lexp_ok"], 1)
                e, s, s2, pl = lruc[:, 3 * w:4 * w], lruc[:, 2 * w:3 * w], lruc[:, w:2 * w], lruc[:, 0:w]
                link(V.tensor_scalar(s, e, 2.0, None, ALU.add))
                link(V.reciprocal(s, s))
                link(V.tensor_tensor(s, e, s, ALU.mult))
                link(V.tensor_tensor(s2, s, s, ALU.mult))
                link(V.tensor_scalar(pl, s2, 1.0 / 19, 1.0 / 17, ALU.mult, ALU.add))
                for k in (15, 13, 11, 9, 7, 5, 3, 1):
                    link(V.tensor_tensor(pl, pl, s2, ALU.mult))
                    link(V.tensor_scalar(pl, pl, 1.0 / k, None, ALU.add))
                link(V.tensor_tensor(pl, pl, s, ALU.mult))
                link(V.tensor_scalar(s, lam, -1.0, 0.0, ALU.mult, ALU.max))
                link(V.scalar_tensor_tensor(out=pl, in0=pl, scalar=2.0, in1=s, op0=ALU.mult, op1=ALU.add))
                link(V.tensor_scalar(pl, pl, LRU_C / 2, None, ALU.mult))
                V.tensor_scalar(lruc[:, w:2 * w], pl, -1.0, None, ALU.mult)
                V.tensor_scalar(lruc[:, 2 * w:3 * w], par[:, PCOL["br"]:PCOL["br"] + w], 0.5, None, ALU.mult)
                V.tensor_scalar(lruc[:, 3 * w:4 * w], par[:, PCOL["bi"]:PCOL["bi"] + w], 0.5, None, ALU.mult)\
                    .then_inc(sm["lruc_ok"], 1)
                dve.wait_ge(sm["lruc_ok"], 1)
                dve.wait_ge(sm["con_in"], 16)

            steps = dict(epi_add=epi_add, epi_relu2=epi_relu2, epi_stage=None, epi_silu=epi_silu,
                         epi_sigm=epi_sigm, epi_proj_a=epi_proj_a, epi_proj_b=epi_proj_b, x_rstd=x_rstd,
                         tail=tail, mk_norm=mk_norm, mq_norm=mq_norm, q_norm=q_norm, k_norm=k_norm,
                         rope2=rope2, att_smx=att_smx, att_prob=att_prob, att_o=att_o, att_lo=att_lo,
                         pool_lo=pool_lo, lru_const=lru_const, conv=conv, lru_square=lru_square, lru=lru, lru_lo=lru_lo,
                         epi_memk=None, epi_memv=None, epi_store=None, epi_store2=None, epi_last=None)

            def run(slab):
                for name, args in sc.steps["dve"].get(slab, ()):
                    if steps[name]:
                        steps[name](*args)

            start()
            x_rstd(0)
            run(-9)
            for kind, g, info in segments():
                if kind == "group":
                    for s in range(S):
                        lo(N(g), s)
                        run(S * g + s)
                else:
                    with dve.Fori(0, NCHUNK - 1) as c:
                        cc = N(0, 1, c)
                        for k in range(8):
                            for s in range(S):
                                lo(cc * 8 + (g + k), s)
                                q = cc * 4 + (info["staged0"] + k)
                                t = cc * 4 + (info["tail0"] + k)
                                if s == 1 and k < 4:
                                    epi_relu2(cc * 8 + (g + k - 1), info["rst"], q, t)
                                if s == 5 and k < 4:
                                    tail(t, 1, 4 * k, None)
                                if s == 1 and k >= 4:
                                    a, done = acc_of(cc * 8 + (g + k - 1))
                                    xs = tokens(x, GW * (k - 4), GW, D)
                                    V.tensor_tensor(xs, two(a), xs, ALU.add).then_inc(done, 1)
            s_, n_ = gout(GALL - 1)
            dve.wait_ge(s_, n_)
            link(V.tensor_reduce(fin_rs, fin_ss.rearrange("p (b n) -> p b n", b=TB), AX.X, ALU.add))
            link(rms(fin_rs, fin_rs, D, TB))
            dve.wait_ge(sm["post_in"], 16)
            dve.wait_ge(sm["x_again"], 16)
            for b in range(TB):
                c = slice(D * b, D * (b + 1))
                link(V.scalar_tensor_tensor(out=y[:, c], in0=y[:, c], scalar=fin_rs[:, b:b + 1], in1=gpost,
                                            op0=ALU.mult, op1=ALU.mult))
                V.tensor_tensor(y[:, c], y[:, c], x[:, c], ALU.add).then_inc(sm["fin_ok"], 1)

        @block.tensor
        def _(pe):
            T = nc.tensor

            def slab(g, s, src, order):
                pe.wait_ge(w_lo, at(g * S + (s + 1)))
                a = acc[g.base % 2]
                if s == 0:
                    if g.base >= 2:
                        pe.wait_ge(out_of[g.base % 2], at(g.half()))
                h, l = sets[src]
                for t in range(SLAB_K):
                    kt = order[s] * SLAB_K + t
                    c = slice((s % RAW) * SLAB + GW * t, (s % RAW) * SLAB + GW * (t + 1))
                    for b in range(TB):
                        tok = slice(TOK * kt + P * b, TOK * kt + P * (b + 1))
                        first, last = s == 0 and t == 0, s == S - 1 and t == SLAB_K - 1
                        o = a[:, GW * b:GW * (b + 1)]
                        T.matmul(o, h[:, tok], whi[:, c], start=first, stop=False)
                        T.matmul(o, h[:, tok], wlo[:, c], start=False, stop=False)
                        ins = T.matmul(o, l[:, tok], whi[:, c], start=False, stop=last)
                ins.then_inc(mm, 1)

            def tail(t, src):
                t = t if isinstance(t, N) else N(t)
                source_ready(pe, src)
                if at_least_one(t):
                    pe.wait_ge(sm["tail_lo"], at(t))
                for j in range(4):
                    for b in range(TB):
                        o = TOK * j + P * b
                        ins = T.transpose(tp[:, o:o + P], source_tile(src, j, b), ident)
                ins.then_inc(sm["tail_tp"], 1)

            def mk_tp(l):
                pe.wait_ge(sm["mk_norm"], at(l + 1))
                if l:
                    pe.wait_ge(sm["pool_lo"], 4)
                for h in range(MH):
                    for b in range(TB):
                        o = TOK * h + P * b
                        ins = T.transpose(sd[:, o:o + P], prob[:, GW * b + MD * h:][:, 0:MD], ident)
                ins.then_inc(sm["mk_tp"], 1)

            def att_in(j):
                if j:
                    pe.wait_ge(sm["att_lo"], at(j))
                if j < DIFJ:
                    l = j // 2
                    pe.wait_ge(sm["mk_t"], at(l + 1))
                    pe.wait_ge(sm["mq_norm"], at(l + 1))
                    for h in range(2):
                        for b in range(TB):
                            c = D * b + POOLW + MD * (2 * (j % 2) + h)
                            ins = T.transpose(sd[:, (2 * h + b) * P:(2 * h + b + 1) * P], u[:, c:c + MD], ident)
                elif j < B2J:
                    h = j - DIFJ
                    pe.wait_ge(sm["q_norm"], 3)
                    pe.wait_ge(sm["k_norm"], at(2 * (h // 4 + 1)))
                    for m in range(2):
                        for b in range(TB):
                            cq = D * b + QKW * m + DK * h
                            ck = 2 * POOLW * b + QKW * m + DK * h
                            o = (2 * m + b) * P
                            T.transpose(sd[0:DK, o:o + P], u[:, cq:cq + DK], ident)
                            ins = T.transpose(sd[0:DK, 4 * P + o:5 * P + o], kv[:, ck:ck + DK], ident)
                else:
                    i = j - B2J
                    pe.wait_ge(sm["rope"], 5)
                    for h in range(2):
                        for b in range(TB):
                            c = D * b + HD2 * (2 * i + h)
                            T.transpose(sd[:, (2 * h + b) * P:(2 * h + b + 1) * P], u[:, c:c + HD2], ident)
                    for b in range(TB):
                        c = GW * b + HD2 * (i // 2)
                        ins = T.transpose(sd[:, (4 + b) * P:(5 + b) * P], mkv[:, c:c + HD2], ident)
                ins.then_inc(sm["att_in"], 1)

            def att_score(j):
                pe.wait_ge(sm["att_qk"], at(j + 1))
                for r in range(4):
                    o = sd[:, TOK * r:TOK * (r + 1)]
                    if j < DIFJ:
                        kt = (2 * (j % 2) + r // 2) * TOK
                        ins = T.matmul(o, qk[:, P * r:P * (r + 1)], mkv[:, kt:kt + TOK], start=True, stop=True)
                    elif j < B2J:
                        m = r // 2
                        kc = 4 * P + 2 * P * m
                        ins = T.matmul(o, qk[0:DK, P * r:P * (r + 1)], qk[0:DK, kc:kc + TOK],
                                       start=True, stop=True)
                    else:
                        ins = T.matmul(o, qk[:, P * r:P * (r + 1)], qk[:, 4 * P:6 * P], start=True, stop=True)
                ins.then_inc(sm["att_score"], 1)

            def att_pt(j):
                pe.wait_ge(sm["att_prob"], at(j + 1))
                for r in range(2 if DIFJ <= j < B2J else 4):
                    for k in range(2):
                        o = (2 * r + k) * P
                        ins = T.transpose(sd[:, o:o + P], prob[:, TOK * r + P * k:][:, 0:P], ident)
                ins.then_inc(sm["att_pt"], 1)

            def att_pv(j):
                pe.wait_ge(sm["att_ptc"], at(j + 1))
                if j < DIFJ:
                    s, n = gout(sc.info["mem"][j // 2] + 1)
                elif j < B2J:
                    s, n = gout(sc.info["kv"][2 * ((j - DIFJ) // 4) + 1])
                else:
                    s, n = gout(sc.info["k2"] + 1)
                pe.wait_ge(s, n)
                for r in range(2 if DIFJ <= j < B2J else 4):
                    for k in range(2):
                        if j < DIFJ:
                            c = 2 * GW + GW * k + MD * (2 * (j % 2) + r // 2)
                            v = mkv[:, c:c + MD]
                        elif j < B2J:
                            c = 2 * POOLW * k + 2 * QKW + DV * (j - DIFJ)
                            v = kv[:, c:c + DV]
                        else:
                            c = 2 * GW + GW * k + HD2 * ((j - B2J) // 2)
                            v = mkv[:, c:c + HD2]
                        ins = T.matmul(sd[:, P * r:P * (r + 1)], qk[:, (2 * r + k) * P:(2 * r + k + 1) * P], v,
                                       start=k == 0, stop=k == 1)
                ins.then_inc(sm["att_pv"], 1)

            def att_ot(j):
                pe.wait_ge(sm["att_o"], at(j + 1))
                for r in range(2 if DIFJ <= j < B2J else 4):
                    ins = T.transpose(sd[:, P * r:P * (r + 1)], ob[:, P * r:P * (r + 1)], ident)
                ins.then_inc(sm["att_ot"], 1)

            def pool_mix(i, g):
                pe.wait_ge(sm["att_lo"], MEMJ + 2)
                if i:
                    pe.wait_ge(sm["pool_lo"], i)
                pe.wait_ge(sm["pm_in"], 16)
                s, n = gout(g)
                pe.wait_ge(s, n)
                s, n = gout(g - 1)
                pe.wait_ge(s, n)
                for t in range(PGT):
                    for b in range(TB):
                        c = D * b + PG * i + P * t
                        m = (TB * i + b) * TOK
                        ins = T.matmul(sd[:, TOK * t:TOK * (t + 1)], u[:, c:c + P], poolm[:, m:m + TOK],
                                       start=b == 0, stop=b == TB - 1)
                ins.then_inc(sm["pool_mix"], 1)

            def pool_mm(i):
                pe.wait_ge(sm["pool_mid"], at(i + 1))
                pe.wait_ge(sm[f"pw{i % 2}_in"], at(16 * (i // 2 + 1)))
                w = pw[:, (i % 2) * PGT * PG:(i % 2 + 1) * PGT * PG]
                for o in range(PGT):
                    for k in range(PGT):
                        ins = T.matmul(sd[:, TOK * o:TOK * (o + 1)], w[:, PG * k + P * o:PG * k + P * (o + 1)],
                                       qk[:, TOK * k:TOK * (k + 1)], start=k == 0, stop=k == PGT - 1)
                ins.then_inc(sm["pool_mm"], 1)

            def gates(n):
                pe.wait_ge(sm["conv_ok"], at(n + 1))
                if n:
                    pe.wait_ge(sm["gates_ok"], at(n))
                pe.wait_ge(sm["att_lo"], NJOB)
                pe.wait_ge(sm[f"lw{n % 2}_in"], at(32 * (n // 2 + 1)))
                for d in range(2):
                    for k in range(2):
                        o = 2 * d + k
                        w = lw[:, ((n % 2) * 4 + o) * P:((n % 2) * 4 + o + 1) * P]
                        ins = T.matmul(sd[:, TOK * o:TOK * (o + 1)], w, xhs[:, TOK * (n % 2):TOK * (n % 2 + 1)], start=True, stop=True)
                ins.then_inc(sm["gates_pe"], 1)

            steps = dict(tail=tail, mk_tp=mk_tp, att_in=att_in, att_score=att_score, att_pt=att_pt,
                         att_pv=att_pv, att_ot=att_ot, pool_mix=pool_mix, pool_mm=pool_mm, gates=gates)

            def run(slab):
                for name, args in sc.steps["pe"].get(slab, ()):
                    steps[name](*args)

            pe.wait_ge(sm["con_in"], 16)
            run(-9)
            for kind, g, info in segments():
                if kind == "group":
                    for s in range(S):
                        for name, count in info.need.get(s, ()):
                            pe.wait_ge(sm[name], at(count))
                        slab(N(g), s, info.src, info.order)
                        run(S * g + s)
                else:
                    order = list(range(S))
                    with pe.Fori(0, NCHUNK - 1) as c:
                        cc = N(0, 1, c)
                        for k, (w, r, col, src) in enumerate(loop_groups(info, cc)):
                            for s in range(S):
                                if k == 3 and s in (0, S - 2):
                                    pe.wait_ge(sm["tail_lo"], at(cc * 4 + (info["tail0"] + (3 if s == 0 else 4))))
                                slab(cc * 8 + (g + k), s, src, order)
                                if s == 3 and k < 4:
                                    tail(cc * 4 + (info["tail0"] + k), ("staged", cc * 4 + (info["staged0"] + k)))


def constants():
    f = np.float32
    const = np.zeros((P, NCON), f)
    const[:, CID:CID + P] = np.eye(P, dtype=f)
    tok = np.arange(TOK)
    q = (np.arange(P)[:, None, None] + P * np.arange(TB)[None, :, None])
    key = tok[None, None, :]
    const[:, CCAUS:CCAUS + 2 * TOK] = np.where(key <= q, f(0), f(-1e30)).reshape(P, -1)
    const[:, CBAND:CBAND + 2 * TOK] = np.where(np.abs(key - q) <= 128, f(0), f(-1e30)).reshape(P, -1)
    for col, half in ((CR1, ROPE1), (CR2, ROPE2)):
        inv = (f(THETA) ** (-(np.arange(half, dtype=f) * f(2)) / f(2 * half))).astype(f)
        ang = (tok.astype(f)[:, None] * inv[None, :]).astype(f).astype(np.float64)
        cs = np.stack([np.cos(ang), np.sin(ang)]).astype(f)
        cs = cs.reshape(2, TB, P, half).transpose(2, 0, 1, 3)
        const[:, col:col + 2 * TB * half] = cs.reshape(P, -1)
    pm = np.zeros((len(WINDOWS), TOK, TOK), f)
    for i, w in enumerate(WINDOWS):
        src, dst = tok[:, None], tok[None, :]
        pm[i] = np.where((src <= dst) & (src > dst - w), f(1) / np.minimum(dst + 1, w).astype(f), f(0))
        pm[i] -= np.eye(TOK, dtype=f)
    pm = pm.reshape(len(WINDOWS), TB, P, TOK).transpose(2, 0, 1, 3).reshape(P, -1)
    return const, np.ascontiguousarray(pm)


def packed(inputs):
    def tiles(a):
        return np.asarray(a).reshape(-1, P).T

    cols = {"mix0": tiles(inputs["mix_norm"][0]), "mix1": tiles(inputs["mix_norm"][1]),
            "ffn0": tiles(inputs["ffn_norm"][0]), "ffn1": tiles(inputs["ffn_norm"][1]),
            "kv": tiles(inputs["kv_norm"]), "mem0": tiles(inputs["mem_norm"][0]),
            "mem1": tiles(inputs["mem_norm"][1]), "pre": tiles(inputs["norm_pre_w_2"][0]),
            "mq0": tiles(inputs["mem_q_norm"][0]), "mq1": tiles(inputs["mem_q_norm"][1]),
            "mk0": tiles(inputs["mem_k_norm"][0]), "mk1": tiles(inputs["mem_k_norm"][1]),
            "subln": tiles(inputs["subln_norm"][0]), "pscale": tiles(inputs["pool_scale"][0]),
            "convw": np.asarray(inputs["conv_w_2"][0]).reshape(4, LB, P).transpose(2, 1, 0).reshape(P, -1),
            "convb": tiles(inputs["conv_b_2"][0]),
            "br": tiles(inputs["lru_b_r_2"][0]), "bi": tiles(inputs["lru_b_i_2"][0]),
            "lam": tiles(inputs["lru_lambda_2"][0])}
    par = np.concatenate([cols[n] for n in PCOL], axis=1)
    row = np.concatenate([np.asarray(inputs["k_norm"]), np.asarray(inputs["q_norm"][0]),
                          np.asarray(inputs["attn_sink_2"][0]), np.asarray(inputs["diff_lambda"][0]).reshape(-1)])
    return np.ascontiguousarray(par), np.tile(row[None, :], (P, 1))


def kernel(**inputs):
    import concourse.bacc as bacc
    from concourse.bass_utils import run_bass_kernel_spmd

    inputs = {n: np.asarray(a) for n, a in inputs.items()}
    const, poolm = constants()
    par, row = packed(inputs)
    arrays = {n: inputs[n] for n in ("x", "mem", "w_in", "w_out", "w_mem_kv", "w_ff1", "w_ff2", "pool_w", "w_kv",
                                     "w_in_2", "lru_w_r_2", "lru_w_i_2", "w_proj_a_2", "w_proj_b_2",
                                     "w_out_2")}
    arrays.update(const=const, poolm=poolm, par=par, row=row,
                  post=np.tile(inputs["norm_post_w_2"][0][None, :], (P, 1)))
    nc = bacc.Bacc("TRN2", target_bir_lowering=False, num_devices=1)
    args, sent = {}, {}
    for n, a in arrays.items():
        sent["in_" + n] = np.ascontiguousarray(a)
        args[n] = nc.dram_tensor("in_" + n, a.shape, mybir.dt.from_np(a.dtype), kind="ExternalInput").ap()
    out = nc.dram_tensor("out", (1, TOK, D), mybir.dt.float32, kind="ExternalOutput").ap()
    build(nc, args, out)
    return run_bass_kernel_spmd(nc, [sent], core_ids=[0]).results[0]["out"]
```

```python
import math
from contextlib import ExitStack

import numpy as np

import concourse.bass as bass
from concourse import mybir

P = 128
TOK = 256
TB = TOK // P
D = 2048
NK = D // P
GW = 512
SLAB_K = 2
NSLAB = NK // SLAB_K
SLAB = SLAB_K * GW
RAW = 4
DFF = 4 * D
NCHUNK = DFF // D
MEMW = 512
MH, MD = 4, 128
POOLW = D - MEMW
WINDOWS = (2, 4, 8, 16)
PG = POOLW // len(WINDOWS)
PGT = PG // P
DH, DK, DV = 12, 64, 128
QKW = DH * DK
LAM_INIT = 0.8 - 0.6 * math.exp(-0.3 * 1)
ROPE1 = DK // 8
H2, HD2, KVH2 = 16, 128, 4
ROPE2 = HD2 // 8
LB = 16
LRU_C = 8.0
EPS = 1e-6
THETA = 500000.0
UTW = TOK + 3

PCOL = {}
_at = 0
for _name, _n in (("mix0", NK), ("mix1", NK), ("ffn0", NK), ("ffn1", NK), ("kv", NK), ("mem0", NK),
                  ("mem1", NK), ("pre", NK), ("mq0", 1), ("mq1", 1), ("mk0", 1), ("mk1", 1), ("subln", 1),
                  ("pscale", POOLW // P), ("convw", 4 * LB), ("convb", LB), ("br", 2 * LB), ("bi", 2 * LB),
                  ("lam", 2 * LB)):
    PCOL[_name] = _at
    _at += _n
NPAR = _at
RKN, RQN, RSINK, RLAM = 0, DK, 2 * DK, 2 * DK + H2
NROW = RLAM + 4 * DK
CID, CMASK0, CCAUS, CBAND = 0, P, P + 2 * TOK, P + 2 * TOK + 3 * P
CR1 = CBAND + 2 * TOK
CR2 = CR1 + 2 * TB * ROPE1
NCON = CR2 + 2 * TB * ROPE2


class N:

    def __init__(self, base, coef=0, reg=None):
        self.base, self.coef, self.reg = base, coef, reg

    def __mul__(self, k):
        return N(self.base * k, self.coef * k, self.reg)

    def __add__(self, k):
        return N(self.base + k, self.coef, self.reg)

    def half(self):
        return N(self.base // 2, self.coef // 2, self.reg)

    @property
    def v(self):
        return self.base if self.reg is None or self.coef == 0 else self.reg * self.coef + self.base


def at_least_one(n):
    return (n.base if isinstance(n, N) else n) > 0


def at(n):
    v = n.v if isinstance(n, N) else n
    assert not isinstance(v, int) or v > 0
    return v


class Group:
    def __init__(self, w, row, col, src, order=None, pieces=None):
        self.w, self.row, self.col, self.src = w, row, col, src
        self.order = order or list(range(NSLAB))
        self.pieces = pieces
        self.need = {}


class Schedule:

    def __init__(self):
        self.groups = []
        self.steps = {e: {} for e in ("pe", "act", "dve", "pool")}
        self.tails = 0
        self.staged = 0
        self.halves = 0
        self.info = {}
        self.norms = []
        self.loops = {}

    def group(self, *a, **k):
        self.groups.append(Group(*a, **k))
        return len(self.groups) - 1

    def at(self, eng, slab, name, *args):
        self.steps[eng].setdefault(slab, []).append((name, args))

    def epilogue(self, g, kind, *args, late=False):
        s = NSLAB * (g + 1)
        self.at("act", s + (2 if late else 1), "epi_" + kind, g, *args)
        self.at("dve", s + (3 if late else 1), "epi_" + kind, g, *args)

    def tail(self, slab_pe, slab_split, source, dst, kt, gain=None):
        t = self.tails
        self.tails += 1
        self.at("pe", slab_pe, "tail", t, source)
        self.at("act", slab_split, "tail", t, dst, kt, gain)
        self.at("dve", slab_split, "tail", t, dst, kt, gain)
        return t

    def attention(self, j, p):
        dif = is_dif(j)
        for name, off in (("in", 0), ("score", 1), ("pt", 5), ("pv", 6)) + ((("ot", 7),) if not dif else ()):
            self.at("pe", p + off, "att_" + name, j)
        for name, off in (("qk", 3), ("exp", 4), ("pt", 8)) + ((("out", 9),) if dif else (("hi", 10),)):
            self.at("act", p + off, "att_" + name, j)
        for name, off in (("smx", 4), ("prob", 5)) + ((("o", 9), ("lo", 10)) if not dif else ()):
            self.at("dve", p + off, "att_" + name, j)

    def norm(self, what, slabs):
        assert all(slabs[0] > b or slabs[-1] < a for a, b in self.norms)
        self.norms.append((slabs[0], slabs[-1]))
        for part, s in zip(("sum", "root", "scale", "rope"), slabs):
            self.at("dve", s, "norm_" + part, *what)


MEMJ, DIFJ = 0, MH // 2
MEM1J = DIFJ + DH
B2J = MEM1J + MH // 2
NJOB = B2J + H2 // 2


def is_dif(j):
    return DIFJ <= j < MEM1J


def row_jobs(j):
    return min(j, DIFJ) if j < MEM1J else j - DH


def plan():
    sc = Schedule()
    S = NSLAB

    g0 = sc.group("w_mem_kv0", 0, 0, 1)
    g1 = sc.group("w_mem_kv0", 0, GW, 1)
    for g, (a, b) in enumerate(((-1, -1), (-1, 0), (0, 2), (2, 4))):
        sc.tail(a, b, ("mem", g), 1, 4 * g, "mem0")
        sc.groups[g0].need[2 * g] = [("tail_lo", g + 1)]
    for i, s in enumerate((3, 5, 6, 7)):
        sc.at("act", s, "x_stat", 0, i)
    sc.at("dve", 8, "x_rstd", 0)
    sc.epilogue(g0, "memk")
    sc.epilogue(g1, "memv")
    for g, (a, b) in enumerate(((7, 9), (9, 11), (12, 14), (15, 17))):
        sc.tail(a, b, ("x0", g), 0, 4 * g, "mix0")
    for i, s in enumerate((10, 12, 13, 15)):
        sc.at("act", s, "x_stat", 1, i)
    sc.at("dve", 18, "x_rstd", 1)
    q = sc.group("w_in0", 0, POOLW, 0)
    sc.groups[q].need[0] = [("tail_lo", sc.tails - 1)]
    sc.groups[q].need[S - 2] = [("tail_lo", sc.tails)]
    sc.at("dve", S * q + 6, "lambda_sums")
    sc.at("act", S * q + 7, "lambda_exps")
    sc.at("dve", S * q + 8, "lambda_done")
    sc.at("dve", S * (q + 6) + 7, "softplus", 0)
    sc.at("dve", S * (q + 7), "softplus", 1)
    us = [sc.group("w_in0", 0, GW * i, 0) for i in range(3)]
    sc.epilogue(q, "store", "u", 1, POOLW)
    for i, g in enumerate(us):
        sc.epilogue(g, "store", "u", 1, GW * i)
    sc.norm(("mk", 0, g0), (S * g1 + 3, S * g1 + 4, S * g1 + 5))
    sc.at("pe", S * q + 3, "mk_tp", 0)
    sc.at("act", S * q + 5, "mk_t", 0)
    sc.norm(("mq", 0, q), (S * us[0] + 2, S * us[0] + 3, S * us[0] + 4))
    sc.attention(MEMJ, S * us[0] + 4)
    sc.attention(MEMJ + 1, S * us[1] + 4)
    out0 = us[2] + 1
    for i, p in enumerate((S * us[2] + 5, S * out0, S * out0 + 2, S * out0 + 4)):
        need = us[(PG * (i + 1) - 1) // GW]
        sc.at("pool", 0, "pool_w", i)
        sc.at("pe", p, "pool_mix", i, need)
        sc.at("act", p + 1, "pool_mid", i)
        sc.at("pe", p + 1, "pool_mm", i)
        sc.at("act", p + 2, "pool_hi", i)
        sc.at("dve", p + 2, "pool_lo", i)

    def project_out(layer, first_order, need, rst_ffn):
        gs = []
        for i in range(4):
            g = sc.group(f"w_out{layer}", 0, GW * i, 1, order=first_order if i == 0 else None)
            gs.append(g)
            if i == 0:
                for s, lst in need.items():
                    sc.groups[g].need[s] = lst
            sc.epilogue(g, "add", GW * i)
            sc.at("act", S * (g + 1) + 1, "x_stat", rst_ffn, i, g)
            sc.tail(S * (g + 1) + 3, S * (g + 1) + 5, ("x", i, g), 0, 4 * i, f"ffn{layer}")
        sc.at("dve", S * (gs[3] + 1) + 2, "x_rstd", rst_ffn)

    def ffn(layer, rst, next_rst, next_dst, next_gain):
        first = sc.group(f"w_ff1{layer}", 0, 0, 0)
        sc.groups[first].need[0] = [("tail_lo", sc.tails - 1)]
        sc.groups[first].need[S - 2] = [("tail_lo", sc.tails)]
        sc.loops[first + 1] = dict(layer=layer, tail0=sc.tails, staged0=sc.staged, rst=rst)
        for _ in range(8 * (NCHUNK - 1)):
            sc.group(None, 0, 0, 0)
        sc.tails += 4 * (NCHUNK - 1)
        sc.staged += 4 * (NCHUNK - 1)
        c = NCHUNK - 1
        prev = len(sc.groups) - 1
        gs = [prev] + [sc.group(f"w_ff1{layer}", 0, D * c + GW * i, 0) for i in range(1, 4)]
        for i, g in enumerate(gs):
            sc.epilogue(g, "relu2", rst, sc.staged, sc.tails)
            sc.tail(S * (g + 1) + 3, S * (g + 1) + 5, ("staged", sc.staged), 1, 4 * i)
            sc.staged += 1
        fs = []
        for i in range(4):
            g = sc.group(f"w_ff2{layer}", D * c, GW * i, 1)
            if i == 0:
                sc.groups[g].need[0] = [("tail_lo", sc.tails - 1)]
                sc.groups[g].need[S - 2] = [("tail_lo", sc.tails)]
            sc.epilogue(g, "add", GW * i)
            sc.at("act", S * (g + 1) + 1, "x_stat", next_rst, i, g)
            fs.append(g)
        for i, g in enumerate(fs):
            sc.tail(S * (g + 1) + 3, S * (g + 1) + 5, ("x", i, g), next_dst, 4 * i, next_gain)
        sc.at("dve", S * (fs[3] + 1) + 2, "x_rstd", next_rst)

    project_out(0, [6, 7, 0, 1, 2, 3, 4, 5],
                {0: [("att_lo", MEMJ + 2)], 2: [("pool_lo", 1)], 3: [("pool_lo", 2)], 5: [("pool_lo", 3)],
                 6: [("pool_lo", 4)]}, 2)
    ffn(0, 2, 3, 0, "mix1")

    q = sc.group("w_in1", 0, POOLW, 0)
    sc.groups[q].need[0] = [("tail_lo", sc.tails - 1)]
    sc.groups[q].need[S - 2] = [("tail_lo", sc.tails)]
    us = [sc.group("w_in1", 0, GW * i, 0) for i in range(3)]
    sc.epilogue(q, "store", "u", 3, POOLW)
    for i, g in enumerate(us):
        sc.epilogue(g, "store", "u", 3, GW * i)
    for i, s in enumerate((S * us[0] + 1, S * us[0] + 5, S * us[1] + 1, S * us[1] + 5)):
        sc.tail(s, s + 2, ("x1", i), 1, 4 * i, "kv")
    sc.norm(("mq", 1, q), [S * us[0] + i for i in (4, 5, 6)])
    sc.norm(("q", 0, us[0]), [S * us[1] + i for i in (4, 5, 6, 8)])
    sc.norm(("q", 1, us[1]), [S * us[2] + i for i in (2, 3, 4, 5)])
    sc.norm(("q", 2, us[2]), [S * (us[2] + 1) + i for i in (2, 4, 5, 6)])
    ks = []
    for i in range(3):
        ks.append(sc.group("w_kv", 0, 256 * i, 1, pieces=True))
        ks.append(sc.group("w_kv", 0, 2 * QKW + GW * i, 1))
    sc.groups[ks[0]].need[0] = [("tail_lo", sc.tails)]
    for i, s in enumerate((S * ks[0] + 1, S * ks[0] + 5, S * ks[1] + 1, S * ks[1] + 5)):
        sc.at("pool", S * q + i, "mem_again", i, sc.tails)
        sc.tail(s, s + 2, ("mem1", i), 0, 4 * i, "mem1")
    for i in range(3):
        sc.epilogue(ks[2 * i], "store2", 3, 256 * i)
        sc.epilogue(ks[2 * i + 1], "store", "kv", 3, 2 * QKW + GW * i)
        sc.norm(("k", i, ks[2 * i]), [S * ks[2 * i + 1] + k for k in (2, 4, 5, 6)])
    m0 = sc.group("w_mem_kv1", 0, 0, 0)
    sc.groups[m0].need[0] = [("tail_lo", sc.tails)]
    m1 = sc.group("w_mem_kv1", 0, GW, 0)
    sc.epilogue(m0, "memk")
    sc.epilogue(m1, "memv")
    sc.info.update(mem=(g0, m0), kv=ks, head_tail=sc.tails)
    for h in range(DH - 1):
        sc.attention(DIFJ + h, S * ks[2] + 3 + 4 * h)
    sc.norm(("sub", 0, None), [S * m0 + k for k in (0, 1, 2)])
    sc.norm(("sub", 1, None), [S * m1 + k for k in (1, 2, 3)])
    sc.norm(("mk", 1, m0), [S * m1 + k for k in (4, 5, 6)])
    w = S * (m1 + 1)
    sc.tail(w - 1, w, ("sub", 0), 1, 0, "subln")
    sc.tail(w, w + 1, ("sub", 1), 1, 4, "subln")
    last, ma, mb = MEM1J - 1, MEM1J, MEM1J + 1
    for e, s, steps in (
            ("pe", w + 1, (("in", last),)), ("pe", w + 2, (("score", last), ("mk_tp", 1))),
            ("pe", w + 3, (("pt", last), ("in", ma), ("pv", last), ("score", ma), ("tail", 2), ("pt", ma),
                           ("pv", ma), ("ot", ma), ("in", mb), ("score", mb))),
            ("pe", w + 4, (("pt", mb),)), ("pe", w + 5, (("pv", mb), ("ot", mb))),
            ("act", w + 3, (("qk", last),)), ("act", w + 4, (("exp", last),)),
            ("act", w + 6, (("mk_t", 1), ("pt", last), ("qk", ma), ("out", last), ("exp", ma))),
            ("act", w + 7, (("tail", 2), ("pt", ma), ("hi", ma), ("qk", mb), ("exp", mb))),
            ("act", w + 8, (("pt", mb),)), ("act", w + 9, (("hi", mb),)),
            ("dve", w + 4, (("smx", last),)), ("dve", w + 5, (("prob", last),)),
            ("dve", w + 6, (("smx", ma), ("sub", 2), ("prob", ma))),
            ("dve", w + 7, (("tail", 2), ("o", ma), ("lo", ma), ("smx", mb), ("prob", mb))),
            ("dve", w + 9, (("o", mb), ("lo", mb)))):
        for name, arg in steps:
            if name == "tail":
                sc.at(e, s, "tail", sc.tails, *((("sub", 2),) if e == "pe" else (1, 8, "subln")))
            elif name == "sub":
                sc.norm(("sub", 2, None), (s, s, s))
            elif name in ("mk_tp", "mk_t"):
                sc.at(e, s, name, arg)
            else:
                sc.at(e, s, "att_" + name, arg)
    sc.tails += 1
    project_out(1, None, {0: [("tail_lo", sc.tails - 2)], 2: [("tail_lo", sc.tails - 1)],
                          4: [("tail_lo", sc.tails)], 6: [("att_lo", row_jobs(B2J))]}, 4)
    ffn(1, 4, 5, 0, "pre")

    qs = [sc.group("w_in_2", 0, 2 * D + GW * i, 0) for i in range(4)]
    sc.groups[qs[0]].need[0] = [("tail_lo", sc.tails - 1)]
    sc.groups[qs[0]].need[S - 2] = [("tail_lo", sc.tails)]
    sc.at("pool", S * (qs[0] + 1) + 6, "x_spill", sc.tails)
    for i, g in enumerate(qs):
        sc.epilogue(g, "store", "u", 5, GW * i, late=True)
        sc.at("dve", S * (g + 1) + 4, "rope2", "u", i, g)
    k = sc.group("w_in_2", 0, 3 * D, 0)
    v = sc.group("w_in_2", 0, 3 * D + GW, 0)
    sc.epilogue(k, "store", "k2", 5, 0, late=True)
    sc.epilogue(v, "store", "v2", 5, 0, late=True)
    sc.at("dve", S * (k + 1) + 4, "rope2", "k2", 0, k)
    sc.info["k2"] = k
    ga = [sc.group("w_in_2", 0, 3 * D + 2 * GW + GW * i, 0) for i in range(4)]
    for i, g in enumerate(ga):
        sc.epilogue(g, "silu", sc.halves, sc.tails, i, 0, late=True)
        sc.at("pool", S * (g + 1) + 3, "gate_store", i, g)
        sc.halves += 1
    ul = [sc.group("w_in_2", 0, GW * i, 0) for i in range(4)]
    sc.info["ut"] = sc.tails
    for i, g in enumerate(ul):
        sc.epilogue(g, "stage", sc.tails, late=True)
        sc.tail(S * (g + 1) + 4, S * (g + 1) + 7, ("out", g), "ut", 4 * i)
    gl = [sc.group("w_in_2", 0, D + GW * i, 0) for i in range(4)]
    for i, g in enumerate(gl):
        sc.epilogue(g, "silu", sc.halves, sc.tails, 4, 0, late=True)
        sc.tail(S * (g + 1) + 4, S * (g + 1) + 7, ("out", g), "gt", 4 * i)
        sc.halves += 1
    for j in range(H2 // 2):
        sc.at("pool", S * (ga[1] + j) + 3, "gate_load", j)
        sc.attention(B2J + j, S * (ga[1] + j) + 4)
    ml = [sc.group("w_in_2", 0, 4 * D + 2 * GW + GW * i, 0) for i in range(8)]
    for i, g in enumerate(ml):
        sc.epilogue(g, "sigm", sc.halves, sc.tails, 4, i, late=True)
        sc.at("pool", S * (g + 1) + 3, "merge_store", i, g)
        sc.halves += 1
    sc.at("dve", S * ul[0] + 2, "lru_const")
    for n in range(LB):
        p = S * gl[2] + 5 * n + 3
        sc.at("pool", p - 8, "lru_w", n)
        sc.at("dve", p - 1, "conv", n)
        sc.at("pe", p, "gates", n)
        sc.at("act", p + 4, "gates", n)
        sc.at("dve", p + 5, "lru_square", n)
        sc.at("act", p + 6, "root", n)
        sc.at("dve", p + 7, "lru", n)
        sc.at("act", p + 8, "lru_hi", n)
        sc.at("dve", p + 9, "lru_lo", n)
    for i in range(4):
        a = sc.group("w_proj_a_2", 0, GW * i, 2)
        b = sc.group("w_proj_b_2", 0, GW * i, 1)
        if i == 0:
            sc.groups[a].need[0] = [("lru_lo", LB - 2)]
            sc.groups[a].need[S - 1] = [("lru_lo", LB)]
            sc.groups[b].need[0] = [("att_lo", row_jobs(NJOB))]
        sc.at("pool", S * a + (4 if i == 0 else 3), "merge_load", i, a)
        sc.epilogue(a, "proj_a", i)
        sc.epilogue(b, "proj_b", sc.tails)
        sc.tail(S * (b + 1) + 3, S * (b + 1) + 5, ("out", b), 0, 4 * i)
    sc.at("pool", S * (b + 1) + 1, "x_back", a)
    for i in range(4):
        g = sc.group("w_out_2", 0, GW * i, 0)
        if i == 0:
            sc.groups[g].need[0] = [("tail_lo", sc.tails - 1)]
            sc.groups[g].need[S - 2] = [("tail_lo", sc.tails)]
        sc.epilogue(g, "last", i)
    return sc


def build(nc, A, out):
    f32, f32r = mybir.dt.float32, mybir.dt.float32r
    ALU, ACT, AX = mybir.AluOpType, mybir.ActivationFunctionType, mybir.AxisListType
    sc = plan()
    S = NSLAB
    GALL = len(sc.groups)
    ctx = ExitStack()
    with ctx:
        place = {}

        def sb(name, cols, dt=f32):
            at = nc.sbuf_base
            place[name] = (at, at + 4 * cols)
            return ctx.enter_context(nc.sbuf_tensor(name, [P, cols], dt))

        def sem(name):
            return ctx.enter_context(nc.semaphore(name))

        raw = sb("raw", RAW * SLAB)
        whi, wlo = sb("whi", RAW * SLAB, f32r), sb("wlo", RAW * SLAB, f32r)
        sets = [(sb("set0_hi", NK * TOK, f32r), sb("set0_lo", NK * TOK, f32r)),
                (sb("set1_hi", NK * TOK, f32r), sb("set1_lo", NK * TOK, f32r))]
        x = sb("x", TB * D)
        u = sb("u", TB * D)
        kv = sb("kv", TB * 2 * POOLW)
        mkv = sb("mkv", 4 * GW)
        stage_a, stage_b = sb("stage_a", TB * GW), sb("stage_b", TB * GW)
        qk = sb("qk", 4 * TOK)
        prob = sb("prob", 4 * TOK)
        ob = sb("ob", 4 * P)
        scan = sb("scan", 2 * TOK)
        const, par, row = sb("const", NCON), sb("par", NPAR), sb("row", NROW)
        small = sb("small", 178)
        prob_b = nc.alloc_sbuf_tensor_at("prob_b", [P, 4 * TOK], f32, offset=place["ob"][0])
        assert place["scan"][0] == place["ob"][1]
        sets.append(tuple(nc.alloc_sbuf_tensor_at(n, [P, NK * TOK], f32r, offset=at[0])
                          for n, at in (("set2_hi", place["x"]), ("set2_lo", place["u"]))))
        poolm = kv[:, 0:8 * TOK]
        mem = kv[:, 8 * TOK:8 * TOK + TB * D]
        pw = kv[:, 8 * TOK:8 * TOK + 2 * PGT * PG]
        ut = kv[:, 0:LB * UTW]
        lw = kv[:, LB * UTW:LB * UTW + 2 * 4 * P]
        ga = kv[:, LB * UTW + 8 * P:LB * UTW + 8 * P + 4 * P]
        addend = kv[:, LB * UTW + 8 * P:LB * UTW + 8 * P + 2 * TOK]
        gt = x
        y = kv[:, 0:TB * D]
        gpost = u[:, 0:D]
        ident = const[:, CID:CID + P]

        SS, RS = 0, 48
        sumsq = [small[:, SS + 8 * k:SS + 8 * k + 8] for k in range(6)]
        rstd = [small[:, RS + 2 * k:RS + 2 * k + 2] for k in range(6)]
        half_rstd = small[:, 60:62]
        nss = small[:, 62:78]
        nrs = small[:, 78:94]
        stats = [[small[:, c:c + 4] for c in cols] for cols in ((94, 98, 102, 110), (162, 166, 170, 174))]
        esink = small[:, 106:110]
        lamv = small[:, 114:118]
        head_gain = small[:, 118:119]
        fin_ss, fin_rs = small[:, 120:128], small[:, 128:130]
        lruc = sb("lruc", 4 * 2 * LB)
        xhs = ob

        acc = [ctx.enter_context(nc.psum_tensor(f"acc{i}", [P, TB * GW], f32)) for i in range(2)]
        tp = ctx.enter_context(nc.psum_tensor("tp", [P, 4 * TOK], f32))
        sd = ctx.enter_context(nc.psum_tensor("sd", [P, 4 * TOK], f32))

        def gain_of(gain, kt):
            c = PCOL.get(gain, 0) + kt
            return head_gain if gain == "subln" else par[:, c:c + 1]

        def odd(j):
            return is_dif(j) and (j - DIFJ) % 2

        def side(j):
            return tp if odd(j) else sd

        def scores(t, j, r):
            if is_dif(j):
                return t[:, 2 * TOK * (r // 2) + P * (r % 2):][:, 0:P * (r % 2 + 1)]
            return t[:, TOK * r:TOK * (r + 1)]

        def qk_of(j):
            return stage_b if odd(j) else qk

        def prob_of(j):
            return prob_b if odd(j) else prob

        x_dram = nc.dram_tensor("x_spill", [P, TB * D], f32, kind="Internal").ap()
        ga_dram = nc.dram_tensor("gate_spill", [P, TB * D], f32, kind="Internal").ap()
        mg_dram = nc.dram_tensor("merge_spill", [P, 8 * TB * GW], f32, kind="Internal").ap()

        ld = [sem(f"slab_loaded{i}") for i in range(RAW)]
        w_hi, w_lo, mm = sem("w_hi"), sem("w_lo"), sem("slab_multiplied")
        out_of = [sem("group_out0"), sem("group_out1")]
        names = ("tail_tp", "tail_hi", "tail_lo", "staged", "x_stat", "rstd_ok", "stage_th",
                 "att_in", "att_qk", "att_score", "att_smx", "att_exp", "att_prob", "att_pt", "att_ptc",
                 "att_pv", "att_o", "att_ot", "att_hi", "att_lo",
                 "mk_norm", "mk_tp", "mk_t", "mq_norm", "q_norm", "k_norm", "rope",
                 "pool_mix", "pool_mid", "pool_mm", "pool_hi", "pool_lo",
                 "conv_ok", "gates_pe", "gates_ok", "lru_sq", "lru_root", "lru_ok",
                 "lru_hi", "lru_lo", "lruc_ok", "lexp_ok",
                 "sub_ok", "lamx_ok", "lame_ok", "dve_step", "act_step", "ysq_ok", "fin_ok", "ut_pad",
                 "mem0_in", "mem1_in", "mem2_in", "mem3_in", "x_in", "ident_in",
                 "con_in", "par_in", "row_in", "pm_in", "pw0_in",
                 "pw1_in", "mem2a_in", "mem2b_in",
                 "x_out", "x_again", "ga_out", "ga_in", "mg_out", "mg_in", "lw0_in", "lw1_in", "post_in",
                 "out_done")
        sm = {n: sem(n) for n in names}
        block = ctx.enter_context(nc.Block())

        W = {}
        for i in range(2):
            for n in ("w_in", "w_out", "w_mem_kv", "w_ff1", "w_ff2"):
                W[f"{n}{i}"] = A[n][i]
        W["w_kv"] = A["w_kv"]
        for n in ("w_in_2", "w_proj_a_2", "w_proj_b_2", "w_out_2"):
            W[n] = A[n][0]

        def tokens(t, lo, n, width):
            return t[:, 0:TB * width].rearrange("p (b n) -> p b n", b=TB)[:, :, lo:lo + n]

        def two(t, n=GW):
            return t[:, 0:TB * n].rearrange("p (b n) -> p b n", b=TB)

        def gout(g):
            g = g if isinstance(g, N) else N(g)
            return out_of[g.base % 2], at(g.half() + 1)

        def loads(g, s):
            per = S // RAW
            pieces = [i for i, info in enumerate(sc.groups) if info.pieces]
            more = per * len([i for i in pieces if i < g.base])
            if g.base in pieces:
                more += s // RAW + 1
            return g * per + (s // RAW + 1 + more * (SLAB_K - 1))

        def segments():
            g = 0
            while g < GALL:
                if g in sc.loops:
                    yield "loop", g, sc.loops[g]
                    g += 8 * (NCHUNK - 1)
                else:
                    yield "group", g, sc.groups[g]
                    g += 1

        def loop_groups(info, c):
            n = info["layer"]
            L = [(f"w_ff1{n}", N(0), c * D + GW * i, 0) for i in range(1, 4)]
            L += [(f"w_ff2{n}", c * D, N(GW * i), 1) for i in range(4)]
            L += [(f"w_ff1{n}", N(0), c * D + D, 0)]
            return L

        def ut_tiles(kt, n):
            return ut.rearrange("p (n t) -> p n t", t=UTW)[:, kt:kt + n, 2:2 + TOK]

        def source_ready(eng, src):
            kind = src[0]
            if kind == "mem":
                eng.wait_ge(sm[f"mem{src[1]}_in"], 16)
            elif kind == "mem1":
                eng.wait_ge(sm["mem2b_in" if src[1] % 2 else "mem2a_in"], at(16 * (src[1] // 2 + 1)))
            elif kind == "sub":
                eng.wait_ge(sm["sub_ok"], at(src[1] + 1))
                eng.wait_ge(sm["att_o"], MEM1J if src[1] == 2 else MEM1J - 2)
            elif kind == "x0":
                eng.wait_ge(sm["x_in"], 16)
            elif kind == "x":
                s, n = gout(src[2])
                eng.wait_ge(s, n)
            elif kind == "out":
                s, n = gout(src[1])
                eng.wait_ge(s, n)
            elif kind == "staged":
                eng.wait_ge(sm["staged"], at(src[1] + 1))

        def source_tile(src, j, b):
            kind = src[0]
            if kind == "mem1":
                return mkv[:, TB * GW * (src[1] % 2) + GW * b + P * j:][:, 0:P]
            if kind == "sub":
                return kv[:, 2 * POOLW * b + 2 * QKW + GW * src[1] + P * j:][:, 0:P]
            if kind == "mem":
                return mem[:, D * b + GW * src[1] + P * j:][:, 0:P]
            if kind in ("x", "x0", "x1"):
                return x[:, D * b + GW * src[1] + P * j:][:, 0:P]
            return stage_b[:, GW * b + P * j:][:, 0:P]

        @block.sync
        def _(sp):
            def slab(g, s, w, row, col, order, pieces=None):
                n = g * S + s
                if n.base >= RAW:
                    sp.wait_ge(w_lo, at(n + (1 - RAW)))
                k = order[s] * SLAB_K * P
                rows = (row + k).v
                dst = raw[:, (s % RAW) * SLAB:(s % RAW + 1) * SLAB]
                if isinstance(rows, int):
                    src = w[rows:rows + SLAB_K * P, :]
                else:
                    src = w[bass.ds(rows, SLAB_K * P), :]
                if pieces:
                    src = src[:, 0:2 * QKW].rearrange("(t p) (m c) -> p t m c", p=P, m=2)
                    dst = dst.rearrange("p (t m c) -> p t m c", t=SLAB_K, m=2)
                    for k in range(SLAB_K):
                        sp.dma_start(dst[:, k], src[:, k, :, col.base:col.base + GW // 2])\
                            .then_inc(ld[s % RAW], 16)
                else:
                    c = col.v
                    src = src[:, c:c + GW] if isinstance(c, int) else src[:, bass.ds(c, GW)]
                    sp.dma_start(dst.rearrange("p (t n) -> p t n", t=SLAB_K),
                                 src.rearrange("(t p) n -> p t n", p=P)).then_inc(ld[s % RAW], 16)

            def memory(i):
                sp.dma_start(tokens(mem, GW * i, GW, D),
                             A["mem"][0].rearrange("(b p) n -> p b n", p=P)[:, :, GW * i:GW * (i + 1)])\
                    .then_inc(sm[f"mem{i}_in"], 16)

            for kind, g, info in segments():
                if kind == "group":
                    for s in range(S):
                        if g == 0 and s < D // GW:
                            memory(s)
                        slab(N(g), s, W[info.w], N(info.row), N(info.col), info.order, info.pieces)
                else:
                    with sp.Fori(0, NCHUNK - 1) as c:
                        cc = N(0, 1, c)
                        for k, (w, r, col, _) in enumerate(loop_groups(info, cc)):
                            for s in range(S):
                                slab(cc * 8 + (g + k), s, W[w], r, col, list(range(S)))
            o = out[0].rearrange("(b p) n -> p b n", p=P)
            for i in range(2 * TB):
                b, c = i // 2, D // 2 * (i % 2)
                sp.wait_ge(sm["fin_ok"], at(i + 1))
                sp.dma_start(o[:, b, c:c + D // 2], y[:, D * b + c:D * b + c + D // 2]).then_inc(sm["out_done"], 16)
            sp.wait_ge(sm["out_done"], 16 * 2 * TB)

        @block.gpsimd
        def _(pool):
            dma = nc.gpsimd.dma_start
            pool.wait_ge(sm["mem3_in"], 16)
            dma(x[:].rearrange("p (b n) -> p b n", b=TB),
                A["x"][0].rearrange("(b p) n -> p b n", p=P)).then_inc(sm["x_in"], 16)
            pool.wait_ge(sm["x_in"], 16)
            dma(poolm, A["poolm"]).then_inc(sm["pm_in"], 16)

            def pool_w(i):
                pool.wait_ge(sm["tail_tp"], 4)
                pool.wait_ge(sm["rstd_ok"], 1)
                if i >= 2:
                    pool.wait_ge(sm["pool_mm"], at(i - 1))
                dst = pw[:, (i % 2) * PGT * PG:(i % 2 + 1) * PGT * PG]
                dma(dst.rearrange("p (t n) -> p t n", t=PGT),
                    A["pool_w"][0, i].rearrange("(t p) n -> p t n", p=P)).then_inc(sm[f"pw{i % 2}_in"], 16)

            def mem_again(i, tails):
                if i < 2:
                    pool.wait_ge(sm["att_lo"], DIFJ)
                else:
                    pool.wait_ge(sm["tail_tp"], at(tails - 1))
                dma(two(mkv[:, TB * GW * (i % 2):TB * GW * (i % 2 + 1)]),
                    A["mem"][0].rearrange("(b p) n -> p b n", p=P)[:, :, GW * i:GW * (i + 1)])\
                    .then_inc(sm["mem2b_in" if i % 2 else "mem2a_in"], 16)

            def x_spill(tails):
                pool.wait_ge(sm["tail_tp"], at(tails))
                pool.wait_ge(sm["rstd_ok"], 6)
                dma(x_dram, x[:]).then_inc(sm["x_out"], 16)

            def gate_store(i, g):
                pool.wait_ge(*gout(g))
                dma(tokens(ga_dram, GW * i, GW, D), two(stage_b)).then_inc(sm["ga_out"], 16)

            def gate_load(j):
                pool.wait_ge(sm["ga_out"], 16 * (j // 2 + 1))
                if j:
                    pool.wait_ge(sm["att_o"], at(B2J + j))
                dma(ga.rearrange("p (b n) -> p b n", b=TB),
                    tokens(ga_dram, 2 * P * j, 2 * P, D)).then_inc(sm["ga_in"], 16)

            def merge_store(i, g):
                pool.wait_ge(*gout(g))
                dma(mg_dram[:, 2 * GW * i:2 * GW * (i + 1)], stage_b[:]).then_inc(sm["mg_out"], 16)

            def merge_load(i, a):
                pool.wait_ge(sm["mg_out"], 128)
                if i == 0:
                    pool.wait_ge(sm["att_lo"], row_jobs(NJOB))
                else:
                    s, n = gout(a - 1)
                    pool.wait_ge(s, n)
                dma(mkv[:, 0:2 * GW], mg_dram[:, 2 * GW * i:2 * GW * (i + 1)]).then_inc(sm["mg_in"], 16)
                dma(mkv[:, 2 * GW:4 * GW], mg_dram[:, 2 * GW * (i + 4):2 * GW * (i + 5)])\
                    .then_inc(sm["mg_in"], 16)

            def lru_w(n):
                if n >= 2:
                    pool.wait_ge(sm["gates_pe"], at(n - 1))
                dst = lw[:, (n % 2) * 4 * P:(n % 2 + 1) * 4 * P].rearrange("p (d k j) -> p d k j", d=2, k=2)
                for k, w in enumerate(("lru_w_r_2", "lru_w_i_2")):
                    dma(dst[:, :, k, :], A[w][0, :, n].rearrange("d i j -> i d j"))\
                        .then_inc(sm[f"lw{n % 2}_in"], 16)

            def x_back(a):
                pool.wait_ge(mm, at(S * (a + 1)))
                pool.wait_ge(sm["x_out"], 16)
                dma(x[:], x_dram).then_inc(sm["x_again"], 16)
                dma(gpost, A["post"]).then_inc(sm["post_in"], 16)

            steps = dict(pool_w=pool_w, mem_again=mem_again, x_spill=x_spill, gate_store=gate_store,
                         gate_load=gate_load, merge_store=merge_store, merge_load=merge_load, lru_w=lru_w,
                         x_back=x_back)
            for s in sorted(sc.steps["pool"]):
                for name, args in sc.steps["pool"][s]:
                    steps[name](*args)

        @block.scalar
        def _(act):
            A_ = nc.scalar.activation
            chain = [0]

            def link(ins):
                chain[0] += 1
                ins.then_inc(sm["act_step"], 1)
                act.wait_ge(sm["act_step"], chain[0])

            def hi(g, s):
                n = g * S + s
                act.wait_ge(ld[s % RAW], at(loads(g, s) * 16))
                if n.base >= RAW:
                    act.wait_ge(mm, at(n + (1 - RAW)))
                c = slice((s % RAW) * SLAB, (s % RAW + 1) * SLAB)
                A_(whi[:, c], raw[:, c], ACT.Copy).then_inc(w_hi, 1)

            def acc_of(g):
                g = g if isinstance(g, N) else N(g)
                act.wait_ge(mm, at(g * S + S))
                return acc[g.base % 2], out_of[g.base % 2]

            def scaled(g, k, dst):
                act.wait_ge(sm["rstd_ok"], at(k + 1))
                a, done = acc_of(g)
                for b in range(TB):
                    ins = A_(dst[b], a[:, GW * b:GW * (b + 1)], ACT.Copy, scale=rstd[k][:, b:b + 1])
                ins.then_inc(done, 1)

            def epi_memk(g):
                scaled(g, 0, [mkv[:, 0:GW], mkv[:, GW:2 * GW]])

            def epi_memv(g):
                scaled(g, 0, [mkv[:, 2 * GW:3 * GW], mkv[:, 3 * GW:4 * GW]])

            def epi_store(g, where, k, col):
                if where == "u":
                    dst = [u[:, D * b + col:D * b + col + GW] for b in range(TB)]
                elif where == "kv":
                    dst = [kv[:, 2 * POOLW * b + col:2 * POOLW * b + col + GW] for b in range(TB)]
                else:
                    o = 0 if where == "k2" else TB * GW
                    dst = [mkv[:, o + GW * b:o + GW * (b + 1)] for b in range(TB)]
                scaled(g, k, dst)

            def epi_store2(g, k, col):
                act.wait_ge(sm["rstd_ok"], at(k + 1))
                a, done = acc_of(g)
                for b in range(TB):
                    dst = kv[:, 2 * POOLW * b:2 * POOLW * b + 2 * QKW]
                    dst = dst.rearrange("p (m c) -> p m c", m=2)[:, :, col:col + GW // 2]
                    ins = A_(dst, a[:, GW * b:GW * (b + 1)].rearrange("p (m c) -> p m c", m=2), ACT.Copy,
                             scale=rstd[k][:, b:b + 1])
                ins.then_inc(done, 1)

            def epi_relu2(g, k, q, tails=None):
                act.wait_ge(sm["rstd_ok"], at(k + 1))
                if at_least_one(q):
                    act.wait_ge(sm["staged"], at(q))
                a, done = acc_of(g)
                for b in range(TB):
                    ins = A_(stage_a[:, GW * b:GW * (b + 1)], a[:, GW * b:GW * (b + 1)], ACT.Relu,
                             scale=rstd[k][:, b:b + 1])
                ins.then_inc(done, 1)

            def epi_stage(g, tails):
                act.wait_ge(sm["tail_tp"], at(tails))
                act.wait_ge(sm["ga_out"], 64)
                scaled(g, 5, [stage_b[:, GW * b:GW * (b + 1)] for b in range(TB)])

            def epi_tanh(g, n, tails, stored, merged):
                act.wait_ge(sm["rstd_ok"], 6)
                act.wait_ge(*gout(g - 1))
                a, _ = acc_of(g)
                for b in range(TB):
                    ins = A_(stage_a[:, GW * b:GW * (b + 1)], a[:, GW * b:GW * (b + 1)], ACT.Tanh,
                             scale=half_rstd[:, b:b + 1])
                ins.then_inc(sm["stage_th"], 1)

            def epi_last(g, i):
                a, _ = acc_of(g)
                for b in range(TB):
                    ins = A_(qk[:, GW * b:GW * (b + 1)], a[:, GW * b:GW * (b + 1)], ACT.Square,
                             accum_out=fin_ss[:, 4 * b + i:4 * b + i + 1])
                ins.then_inc(sm["ysq_ok"], 1)

            def x_stat(k, i, g=None):
                if g is not None:
                    s, n = gout(g)
                    act.wait_ge(s, n)
                elif k == 0:
                    act.wait_ge(sm[f"mem{i}_in"], 16)
                else:
                    act.wait_ge(sm["x_in"], 16)
                if 4 * k + i:
                    act.wait_ge(sm["x_stat"], 4 * k + i)
                t = x if k else mem
                for b in range(TB):
                    ins = A_(qk[:, GW * b:GW * (b + 1)], t[:, D * b + GW * i:D * b + GW * (i + 1)],
                             ACT.Square, accum_out=sumsq[k][:, 4 * b + i:4 * b + i + 1])
                ins.then_inc(sm["x_stat"], 1)

            def tail(t, dst, kt, gain):
                t = t if isinstance(t, N) else N(t)
                act.wait_ge(sm["tail_tp"], at(t + 1))
                if dst == "ut":
                    ins = A_(ut_tiles(kt, 2), tp[:, 0:2 * TOK].rearrange("p (n t) -> p n t", n=2), ACT.Copy)
                elif dst == "gt":
                    act.wait_ge(sm["x_out"], 16)
                    ins = A_(gt[:, TOK * kt:TOK * (kt + 2)], tp[:, 0:2 * TOK], ACT.Copy)
                elif gain is None:
                    ins = A_(sets[dst][0][:, TOK * kt:TOK * (kt + 4)], tp[:], ACT.Copy)
                else:
                    for j in range(4):
                        ins = A_(sets[dst][0][:, TOK * (kt + j):TOK * (kt + j + 1)],
                                 tp[:, TOK * j:TOK * (j + 1)], ACT.Copy, scale=gain_of(gain, kt + j))
                ins.then_inc(sm["tail_hi"], 1)

            def mk_t(l):
                act.wait_ge(sm["mk_tp"], at(l + 1))
                A_(mkv[:, 0:4 * TOK], sd[:], ACT.Copy,
                   scale=par[:, PCOL[f"mk{l}"]:PCOL[f"mk{l}"] + 1]).then_inc(sm["mk_t"], 1)

            def att_qk(j):
                act.wait_ge(sm["att_in"], at(j + 1))
                src, dst = side(j), qk_of(j)
                if is_dif(j):
                    ins = A_(dst[0:DK, :], src[0:DK, :], ACT.Copy)
                elif j < B2J:
                    c = PCOL["mq0" if j < DIFJ else "mq1"]
                    ins = A_(dst[:, 0:2 * TOK], src[:, 0:2 * TOK], ACT.Copy, scale=par[:, c:c + 1])
                else:
                    ins = A_(dst[:, 0:3 * TOK], src[:, 0:3 * TOK], ACT.Copy)
                ins.then_inc(sm["att_qk"], 1)

            def att_exp(j):
                act.wait_ge(sm["att_smx"], at(j + 1))
                if j >= B2J:
                    A_(esink, esink, ACT.Exp)
                _, nmx, den, _ = stats[odd(j)]
                for r in range(4):
                    pr = scores(prob_of(j), j, r)
                    ins = A_(pr, pr, ACT.Exp, bias=nmx[:, r:r + 1], accum_out=den[:, r:r + 1])
                ins.then_inc(sm["att_exp"], 1)

            def att_pt(j):
                act.wait_ge(sm["att_pt"], at(j + 1))
                n = 3 * P if is_dif(j) else 4 * TOK
                A_(qk_of(j)[:, 0:n], side(j)[:, 0:n], ACT.Copy).then_inc(sm["att_ptc"], 1)

            def att_out(j):
                act.wait_ge(sm["att_pv"], at(j + 1))
                A_(tokens(kv, 2 * QKW + DV * (j - DIFJ), DV, 2 * POOLW), two(side(j)[:, 0:TB * DV], DV), ACT.Copy)\
                    .then_inc(sm["att_o"], 1)

            def att_dst(j):
                return NK - MH + 2 * (j % 2) if j < B2J else 2 * (j - B2J)

            def att_hi(j):
                act.wait_ge(sm["att_ot"], at(row_jobs(j) + 1))
                kt = att_dst(j)
                A_(sets[1][0][:, TOK * kt:TOK * (kt + 2)], sd[:, 0:2 * TOK], ACT.Copy).then_inc(sm["att_hi"], 1)

            def pool_mid(i):
                act.wait_ge(sm["pool_mix"], at(i + 1))
                A_(qk[:, 0:PGT * TOK], sd[:, 0:PGT * TOK], ACT.Copy).then_inc(sm["pool_mid"], 1)

            def pool_hi(i):
                act.wait_ge(sm["pool_mm"], at(i + 1))
                for t in range(PGT):
                    kt = PGT * i + t
                    c = PCOL["pscale"] + kt
                    ins = A_(sets[1][0][:, TOK * kt:TOK * (kt + 1)], sd[:, TOK * t:TOK * (t + 1)], ACT.Copy,
                             scale=par[:, c:c + 1])
                ins.then_inc(sm["pool_hi"], 1)

            def gates(n):
                act.wait_ge(sm["gates_pe"], at(n + 1))
                act.wait_ge(sm["lruc_ok"], 1)
                if n:
                    act.wait_ge(sm["lru_ok"], at(n))
                for d in range(2):
                    for k in range(2):
                        c = (2 + k) * 2 * LB + LB * d + n
                        o = (2 * k + d) * TOK
                        ins = A_(prob[:, o:o + TOK], sd[:, (2 * d + k) * TOK:(2 * d + k + 1) * TOK],
                                 ACT.Tanh, bias=lruc[:, c:c + 1], scale=0.5)
                link(ins)
                for d in range(2):
                    th = prob[:, d * TOK:(d + 1) * TOK]
                    c, m = LB * d + n, 2 * LB + LB * d + n
                    A_(qk[:, d * TOK:(d + 1) * TOK], th, ACT.Exp,
                       bias=lruc[:, m:m + 1], scale=lruc[:, m:m + 1])
                    ins = A_(qk[:, (2 + d) * TOK:(3 + d) * TOK], th, ACT.Tanh,
                             bias=lruc[:, c:c + 1], scale=lruc[:, c:c + 1])
                ins.then_inc(sm["gates_ok"], 1)

            def root(n):
                act.wait_ge(sm["lru_sq"], n + 1)
                A_(addend, addend, ACT.Sqrt, scale=0.25).then_inc(sm["lru_root"], 1)

            def lru_hi(n):
                act.wait_ge(sm["lru_ok"], at(n + 1))
                A_(sets[2][0][:, TOK * n:TOK * (n + 1)], scan[:, 0:TOK], ACT.Copy).then_inc(sm["lru_hi"], 1)

            def lambda_exps():
                act.wait_ge(sm["lamx_ok"], 1)
                A_(lamv[:, 2:4], lamv[:, 0:2], ACT.Exp).then_inc(sm["lame_ok"], 1)
                A_(lruc[:, 6 * LB:8 * LB], lruc[:, 0:2 * LB], ACT.Exp, scale=-1.0).then_inc(sm["lexp_ok"], 1)

            steps = dict(lambda_exps=lambda_exps, epi_memk=epi_memk, epi_memv=epi_memv,
                         epi_store=epi_store, epi_store2=epi_store2,
                         epi_relu2=epi_relu2, epi_stage=epi_stage, epi_silu=epi_tanh, epi_sigm=epi_tanh,
                         epi_last=epi_last, x_stat=x_stat, tail=tail, mk_t=mk_t, att_qk=att_qk,
                         att_exp=att_exp, att_pt=att_pt, att_out=att_out, att_hi=att_hi,
                         pool_mid=pool_mid, pool_hi=pool_hi,
                         gates=gates, root=root, lru_hi=lru_hi, epi_add=None, epi_proj_a=None, epi_proj_b=None)

            def run(slab):
                for name, args in sc.steps["act"].get(slab, ()):
                    if steps[name]:
                        steps[name](*args)

            act.dma_start(ident, A["const"][:, CID:CID + P]).then_inc(sm["ident_in"], 16)
            act.dma_start(par[:], A["par"]).then_inc(sm["par_in"], 16)
            act.dma_start(row[:], A["row"]).then_inc(sm["row_in"], 16)
            act.dma_start(const[:, P:NCON], A["const"][:, P:NCON]).then_inc(sm["con_in"], 16)
            act.wait_ge(sm["par_in"], 16)
            run(-1)
            for kind, g, info in segments():
                if kind == "group":
                    for s in range(S):
                        hi(N(g), s)
                        run(S * g + s)
                else:
                    with act.Fori(0, NCHUNK - 1) as c:
                        cc = N(0, 1, c)
                        for k in range(8):
                            for s in range(S):
                                hi(cc * 8 + (g + k), s)
                                q = cc * 4 + (info["staged0"] + k)
                                t = cc * 4 + (info["tail0"] + k)
                                if s == 1 and k < 4:
                                    epi_relu2(cc * 8 + (g + k - 1), info["rst"], q, t)
                                if s == 5 and k < 4:
                                    tail(t, 1, 4 * k, None)
            run(S * GALL + 1)

        @block.vector
        def _(dve):
            V = nc.vector
            chain = [0]

            def link(ins):
                chain[0] += 1
                ins.then_inc(sm["dve_step"], 1)
                dve.wait_ge(sm["dve_step"], chain[0])

            def lo(g, s):
                dve.wait_ge(w_hi, at(g * S + (s + 1)))
                c = slice((s % RAW) * SLAB, (s % RAW + 1) * SLAB)
                V.tensor_tensor(wlo[:, c], raw[:, c], whi[:, c].bitcast(f32), ALU.subtract).then_inc(w_lo, 1)

            def acc_of(g):
                g = g if isinstance(g, N) else N(g)
                dve.wait_ge(mm, at(g * S + S))
                return acc[g.base % 2], out_of[g.base % 2]

            def rms(dst, ssq, n, count):
                v, h = small[:, 130:130 + count], small[:, 146:146 + count]
                i32 = mybir.dt.int32
                link(V.tensor_scalar(v, ssq, 1.0 / n, EPS, ALU.mult, ALU.add))
                link(V.tensor_scalar(h.bitcast(i32), v.bitcast(i32), 1, None, ALU.logical_shift_right))
                link(V.tensor_scalar(dst.bitcast(i32), h.bitcast(i32), -1.0, float(0x5F3759DF), ALU.mult,
                                     ALU.add))
                for k in range(3):
                    link(V.tensor_tensor(h, dst, v, ALU.mult))
                    link(V.scalar_tensor_tensor(out=h, in0=h, scalar=-0.5, in1=dst, op0=ALU.mult, op1=ALU.mult))
                    ins = V.scalar_tensor_tensor(out=dst, in0=h, scalar=1.5, in1=dst, op0=ALU.add, op1=ALU.mult)
                    if k < 2:
                        link(ins)
                return ins

            def epi_add(g, col):
                a, done = acc_of(g)
                xs = tokens(x, col, GW, D)
                V.tensor_tensor(xs, two(a), xs, ALU.add).then_inc(done, 1)

            def epi_relu2(g, k, q, tails):
                dve.wait_ge(*gout(g))
                dve.wait_ge(sm["tail_tp"], at(tails))
                V.tensor_tensor(stage_b[:], stage_a[:], stage_a[:], ALU.mult).then_inc(sm["staged"], 1)

            def stage_b_free(tails, stored, merged):
                dve.wait_ge(sm["tail_tp"], at(tails))
                if stored:
                    dve.wait_ge(sm["ga_out"], at(16 * stored))
                if merged:
                    dve.wait_ge(sm["mg_out"], at(16 * merged))

            def epi_silu(g, n, tails, stored, merged):
                dve.wait_ge(sm["stage_th"], at(n + 1))
                stage_b_free(tails, stored, merged)
                a, done = acc_of(g)
                link(V.tensor_scalar(stage_a[:], stage_a[:], 1.0, None, ALU.add))
                for b in range(TB):
                    c = slice(GW * b, GW * (b + 1))
                    ins = V.scalar_tensor_tensor(out=stage_b[:, c], in0=a[:, c], scalar=half_rstd[:, b:b + 1],
                                                 in1=stage_a[:, c], op0=ALU.mult, op1=ALU.mult)
                ins.then_inc(done, 1)

            def epi_sigm(g, n, tails, stored, merged):
                dve.wait_ge(sm["stage_th"], at(n + 1))
                stage_b_free(tails, stored, merged)
                V.tensor_scalar(stage_b[:], stage_a[:], 0.5, 0.5, ALU.mult, ALU.add).then_inc(out_of[g % 2], 1)

            def epi_proj_a(g, i):
                dve.wait_ge(sm["mg_in"], at(32 * (i + 1)))
                a, done = acc_of(g)
                V.tensor_tensor(stage_a[:], a[:], mkv[:, 0:2 * GW], ALU.mult).then_inc(done, 1)

            def epi_proj_b(g, tails):
                a, done = acc_of(g)
                stage_b_free(tails, 4, 8)
                link(V.tensor_tensor(stage_b[:], a[:], mkv[:, 2 * GW:4 * GW], ALU.mult))
                V.tensor_tensor(stage_b[:], stage_b[:], stage_a[:], ALU.add).then_inc(done, 1)

            def x_rstd(k):
                dve.wait_ge(sm["x_stat"], at(4 * (k + 1)))
                link(V.tensor_reduce(rstd[k], sumsq[k].rearrange("p (b n) -> p b n", b=TB), AX.X, ALU.add))
                if k == 5:
                    link(rms(rstd[k], rstd[k], D, TB))
                    V.tensor_scalar(half_rstd, rstd[k], 0.5, None, ALU.mult).then_inc(sm["rstd_ok"], 1)
                else:
                    rms(rstd[k], rstd[k], D, TB).then_inc(sm["rstd_ok"], 1)

            def tail(t, dst, kt, gain):
                t = t if isinstance(t, N) else N(t)
                dve.wait_ge(sm["tail_hi"], at(t + 1))
                if dst == "ut":
                    V.tensor_copy(ut_tiles(kt + 2, 2), tp[:, 2 * TOK:4 * TOK].rearrange("p (n t) -> p n t", n=2))\
                        .then_inc(sm["tail_lo"], 1)
                    return
                if dst == "gt":
                    V.tensor_copy(gt[:, TOK * (kt + 2):TOK * (kt + 4)], tp[:, 2 * TOK:4 * TOK])\
                        .then_inc(sm["tail_lo"], 1)
                    return
                h, l = sets[dst]
                if gain is None:
                    c = slice(TOK * kt, TOK * (kt + 4))
                    ins = V.tensor_tensor(l[:, c], tp[:], h[:, c].bitcast(f32), ALU.subtract)
                else:
                    for j in range(4):
                        c = slice(TOK * (kt + j), TOK * (kt + j + 1))
                        ins = V.scalar_tensor_tensor(out=l[:, c], in0=tp[:, TOK * j:TOK * (j + 1)],
                                                     scalar=gain_of(gain, kt + j), in1=h[:, c].bitcast(f32),
                                                     op0=ALU.mult, op1=ALU.subtract)
                ins.then_inc(sm["tail_lo"], 1)

            def headwise(kind, i):
                if kind == "mk":
                    return [mkv[:, GW * b:GW * (b + 1)].rearrange("p (h d) -> p h d", d=MD) for b in range(TB)], \
                        MD, None, sm["mk_norm"]
                if kind == "mq":
                    return [u[:, D * b + POOLW:D * (b + 1)].rearrange("p (h d) -> p h d", d=MD)
                            for b in range(TB)], MD, None, sm["mq_norm"]
                if kind == "q":
                    return [u[:, D * b + GW * i:D * b + GW * (i + 1)].rearrange("p (h d) -> p h d", d=DK)
                            for b in range(TB)], DK, RQN, sm["q_norm"]
                if kind == "k":
                    return [kv[:, 2 * POOLW * b:2 * POOLW * b + 2 * QKW]
                            .rearrange("p (m c) -> p m c", m=2)[:, :, 256 * i:256 * (i + 1)]
                            .rearrange("p m (h d) -> p m h d", d=DK) for b in range(TB)], DK, RKN, sm["k_norm"]
                return [kv[:, 2 * POOLW * b + 2 * QKW + GW * i:2 * POOLW * b + 2 * QKW + GW * (i + 1)]
                        .rearrange("p (h d) -> p h d", d=DV) for b in range(TB)], DV, None, sm["sub_ok"]

            def per_head(t, like, width):
                heads = list(like.shape[1:-1])
                if width:
                    for _ in heads:
                        t = t.unsqueeze(1)
                    return t.broadcast_to([P] + heads + [width])
                if len(heads) == 2:
                    t = t.rearrange("p (m h) -> p m h", m=heads[0])
                return t.unsqueeze(len(heads) + 1).broadcast_to(list(like.shape))

            def norm_sum(kind, i, g):
                if g is None:
                    dve.wait_ge(sm["att_o"], DIFJ + 4 * (i + 1))
                else:
                    dve.wait_ge(*gout(g))
                views, d, _, _ = headwise(kind, i)
                for b, t in enumerate(views):
                    tmp = stage_a[:, GW * b:GW * (b + 1)]
                    if len(t.shape) == 4:
                        tmp = tmp.rearrange("p (m h d) -> p m h d", m=2, d=d)
                    else:
                        tmp = tmp.rearrange("p (h d) -> p h d", d=d)
                    ins = V.tensor_tensor(tmp, t, t, ALU.mult)
                link(ins)
                n = TB * GW // d
                link(V.tensor_reduce(nss[:, 0:n], stage_a[:].rearrange("p (n d) -> p n d", d=d), AX.X, ALU.add))

            def norm_root(kind, i, g):
                _, d, _, _ = headwise(kind, i)
                n = TB * GW // d
                link(rms(nrs[:, 0:n], nss[:, 0:n], d, n))

            def norm_scale(kind, i, g):
                views, d, gain, told = headwise(kind, i)
                n = GW // d
                for b, t in enumerate(views):
                    ins = V.tensor_tensor(t, t, per_head(nrs[:, n * b:n * (b + 1)], t, None), ALU.mult)
                if gain is None:
                    ins.then_inc(told, 1)
                    return
                link(ins)
                for t in views:
                    ins = V.tensor_tensor(t, t, per_head(row[:, gain:gain + DK], t, DK), ALU.mult)
                link(ins)

            def norm_rope(kind, i, g):
                views, _, _, told = headwise(kind, i)
                rope(views, ROPE1, CR1).then_inc(told, 1)
                dve.wait_ge(told, i + 1)

            def rope(views, half, ccol):
                cs = const[:, ccol:ccol + 2 * TB * half].rearrange("p (k b n) -> p k b n", k=2, b=TB)
                heads = list(views[0].shape[1:-1])
                n = math.prod(heads) * half
                tmp = []
                for i in range(4 * TB):
                    t = stage_a[:, n * i:n * (i + 1)]
                    if len(heads) == 2:
                        tmp.append(t.rearrange("p (m h d) -> p m h d", m=heads[0], d=half))
                    else:
                        tmp.append(t.rearrange("p (h d) -> p h d", d=half))
                for b, t in enumerate(views):
                    t1, t2 = t[..., 0:half], t[..., half:2 * half]
                    c_, s_ = per_head(cs[:, 0, b, :], t, half), per_head(cs[:, 1, b, :], t, half)
                    V.tensor_tensor(tmp[4 * b], t1, c_, ALU.mult)
                    V.tensor_tensor(tmp[4 * b + 1], t2, s_, ALU.mult)
                    V.tensor_tensor(tmp[4 * b + 2], t1, s_, ALU.mult)
                    ins = V.tensor_tensor(tmp[4 * b + 3], t2, c_, ALU.mult)
                link(ins)
                for b, t in enumerate(views):
                    V.tensor_tensor(t[..., 0:half], tmp[4 * b], tmp[4 * b + 1], ALU.subtract)
                    ins = V.tensor_tensor(t[..., half:2 * half], tmp[4 * b + 2], tmp[4 * b + 3], ALU.add)
                return ins

            def rope2(where, i, g):
                dve.wait_ge(*gout(g))
                if where == "u":
                    rows = [u[:, D * b + GW * i:D * b + GW * (i + 1)] for b in range(TB)]
                else:
                    rows = [mkv[:, GW * b:GW * (b + 1)] for b in range(TB)]
                rope([t.rearrange("p (h d) -> p h d", d=HD2) for t in rows], ROPE2, CR2).then_inc(sm["rope"], 1)

            def att_smx(j):
                dve.wait_ge(sm["att_score"], at(j + 1))
                pr, ps = prob_of(j), side(j)
                mx, nmx, _, _ = stats[odd(j)]
                if is_dif(j):
                    dve.wait_ge(sm["att_pt"], at(max(j - 1, DIFJ)))
                    dve.wait_ge(sm["att_ot"], DIFJ)
                    p3 = pr[:].rearrange("p (m n) -> p m n", m=2)[:, :, 0:3 * P]
                    s3 = ps[:].rearrange("p (m n) -> p m n", m=2)[:, :, 0:3 * P]
                    mk = const[:, CCAUS:CCAUS + 3 * P]
                    for m in range(2):
                        ins = V.scalar_tensor_tensor(out=p3[:, m], in0=s3[:, m], scalar=DK ** -0.5, in1=mk,
                                                     op0=ALU.mult, op1=ALU.add)
                    link(ins)
                    m3 = mx.rearrange("p (m b) -> p m b", b=TB)
                    V.tensor_reduce(m3[:, :, 0], p3[:, :, 0:P], AX.X, ALU.max)
                    link(V.tensor_reduce(m3[:, :, 1], p3[:, :, P:3 * P], AX.X, ALU.max))
                    V.tensor_scalar(nmx, mx, -1.0, None, ALU.mult).then_inc(sm["att_smx"], 1)
                    return
                if j:
                    dve.wait_ge(sm["att_pt"], at(j))
                m, scale = (CMASK0, MD ** -0.5) if j < B2J else (CBAND, HD2 ** -0.5)
                pr = prob[:].rearrange("p (r n) -> p r n", r=2)
                ps = sd[:].rearrange("p (r n) -> p r n", r=2)
                mk = const[:, m:m + 2 * TOK]
                for r in range(2):
                    ins = V.scalar_tensor_tensor(out=pr[:, r], in0=ps[:, r], scalar=scale, in1=mk,
                                                 op0=ALU.mult, op1=ALU.add)
                link(ins)
                link(V.tensor_reduce(mx, prob[:].rearrange("p (r n) -> p r n", r=4), AX.X, ALU.max))
                if j >= B2J:
                    sk = row[:, RSINK + 2 * (j - B2J):RSINK + 2 * (j - B2J) + 2]
                    sk = sk.unsqueeze(2).broadcast_to([P, 2, TB])
                    link(V.tensor_tensor(mx.rearrange("p (h b) -> p h b", b=TB),
                                         mx.rearrange("p (h b) -> p h b", b=TB), sk, ALU.max))
                    link(V.tensor_tensor(esink.rearrange("p (h b) -> p h b", b=TB), sk,
                                         mx.rearrange("p (h b) -> p h b", b=TB), ALU.subtract))
                V.tensor_scalar(nmx, mx, -1.0, None, ALU.mult).then_inc(sm["att_smx"], 1)

            def att_prob(j):
                dve.wait_ge(sm["att_exp"], at(j + 1))
                _, _, den, rden = stats[odd(j)]
                if j >= B2J:
                    link(V.tensor_tensor(den, den, esink, ALU.add))
                if not is_dif(j):
                    V.reciprocal(rden, den).then_inc(sm["att_prob"], 1)
                    return
                link(V.reciprocal(rden, den))
                link(V.tensor_scalar(rden[:, 2:4], rden[:, 2:4], lamv[:, 2:3], None, ALU.mult))
                pr = prob_of(j)
                for b in range(TB):
                    c2 = scores(pr, j, 2 + b)
                    ins = V.tensor_scalar(c2, c2, rden[:, 2 + b:3 + b], None, ALU.mult)
                link(ins)
                for b in range(TB):
                    c1 = scores(pr, j, b)
                    ins = V.scalar_tensor_tensor(out=c1, in0=c1, scalar=rden[:, b:b + 1],
                                                 in1=scores(pr, j, 2 + b), op0=ALU.mult, op1=ALU.add)
                ins.then_inc(sm["att_prob"], 1)

            def att_o(j):
                dve.wait_ge(sm["att_pv"], at(j + 1))
                if j:
                    dve.wait_ge(sm["att_ot"], at(row_jobs(j)))
                rden = stats[0][3]
                r = rden.unsqueeze(2).broadcast_to([P, 4, P])
                o4 = ob[:].rearrange("p (r d) -> p r d", r=4)
                ins = V.tensor_tensor(o4, sd[:, 0:4 * P].rearrange("p (r d) -> p r d", r=4), r, ALU.mult)
                if j >= B2J:
                    link(ins)
                    dve.wait_ge(sm["ga_in"], at(16 * (j - B2J + 1)))
                    g4 = ga.rearrange("p (b h d) -> p b h d", b=TB, h=2)
                    for h in range(2):
                        oo = ob[:, 2 * P * h:2 * P * (h + 1)].rearrange("p (b d) -> p b d", b=TB)
                        ins = V.tensor_tensor(oo, oo, g4[:, :, h, :], ALU.mult)
                ins.then_inc(sm["att_o"], 1)

            def att_lo(j):
                dve.wait_ge(sm["att_hi"], at(row_jobs(j) + 1))
                kt = NK - MH + 2 * (j % 2) if j < B2J else 2 * (j - B2J)
                c = slice(TOK * kt, TOK * (kt + 2))
                h, l = sets[1]
                V.tensor_tensor(l[:, c], sd[:, 0:2 * TOK], h[:, c].bitcast(f32), ALU.subtract)\
                    .then_inc(sm["att_lo"], 1)

            def pool_lo(i):
                dve.wait_ge(sm["pool_hi"], at(i + 1))
                h, l = sets[1]
                for t in range(PGT):
                    kt = PGT * i + t
                    c = slice(TOK * kt, TOK * (kt + 1))
                    p = PCOL["pscale"] + kt
                    ins = V.scalar_tensor_tensor(out=l[:, c], in0=sd[:, TOK * t:TOK * (t + 1)],
                                                 scalar=par[:, p:p + 1], in1=h[:, c].bitcast(f32),
                                                 op0=ALU.mult, op1=ALU.subtract)
                ins.then_inc(sm["pool_lo"], 1)

            def lru_const():
                pad = ut.rearrange("p (n t) -> p n t", t=UTW)
                V.memset(pad[:, :, 0:2], 0.0)
                V.memset(pad[:, :, UTW - 1:UTW], 0.0).then_inc(sm["ut_pad"], 1)

            def conv(n):
                dve.wait_ge(sm["tail_hi"], at(sc.info["ut"] + n // 4 + 1))
                dve.wait_ge(sm["tail_lo"], sc.info["ut"] + n // 4 + 1)
                dve.wait_ge(sm["ut_pad"], 1)
                if n >= 2:
                    dve.wait_ge(sm["gates_pe"], at(n - 1))
                dve.wait_ge(sm["att_ot"], row_jobs(NJOB))
                xh = xhs[:, TOK * (n % 2):TOK * (n % 2 + 1)]
                base = UTW * n
                pc = PCOL["convw"] + 4 * n
                link(V.tensor_scalar(xh, ut[:, base:base + TOK], par[:, pc:pc + 1],
                                     par[:, PCOL["convb"] + n:PCOL["convb"] + n + 1], ALU.mult, ALU.add))
                for k in range(1, 4):
                    ins = V.scalar_tensor_tensor(out=xh, in0=ut[:, base + k:base + k + TOK],
                                                 scalar=par[:, pc + k:pc + k + 1], in1=xh,
                                                 op0=ALU.mult, op1=ALU.add)
                    if k < 3:
                        link(ins)
                ins.then_inc(sm["conv_ok"], 1)

            def lru_square(n):
                dve.wait_ge(sm["gates_ok"], at(n + 1))
                if n:
                    dve.wait_ge(sm["lru_lo"], at(n))
                dve.wait_ge(sm["att_o"], NJOB)
                xh = xhs[:, TOK * (n % 2):TOK * (n % 2 + 1)]
                Tt = qk[:, 2 * TOK:4 * TOK]
                link(V.tensor_tensor(scan[:], qk[:, 0:2 * TOK], qk[:, 0:2 * TOK], ALU.mult))
                for d in range(2):
                    c = slice((2 + d) * TOK, (3 + d) * TOK)
                    ins = V.scalar_tensor_tensor(out=prob[:, c], in0=prob[:, c], scalar=1.0, in1=xh,
                                                 op0=ALU.add, op1=ALU.mult)
                V.scalar_tensor_tensor(out=addend, in0=scan[:], scalar=1.0, in1=Tt, op0=ALU.add,
                                       op1=ALU.mult).then_inc(sm["lru_sq"], 1)

            def lru(n):
                dve.wait_ge(sm["lru_root"], n + 1)
                link(V.tensor_tensor(addend, addend, prob[:, 2 * TOK:4 * TOK], ALU.mult))
                V.tensor_tensor_scan(scan[:, 0:TOK], qk[:, 0:TOK], addend[:, 0:TOK], 0.0, ALU.mult, ALU.add)
                link(V.tensor_tensor_scan(scan[:, TOK:2 * TOK][:, ::-1], qk[:, TOK:2 * TOK][:, ::-1],
                                          addend[:, TOK:2 * TOK][:, ::-1], 0.0, ALU.mult, ALU.add))
                link(V.tensor_tensor(scan[:, 0:TOK], scan[:, 0:TOK], scan[:, TOK:2 * TOK], ALU.add))
                V.tensor_tensor(scan[:, 0:TOK], scan[:, 0:TOK], gt[:, TOK * n:TOK * (n + 1)], ALU.mult)\
                    .then_inc(sm["lru_ok"], 1)

            def lru_lo(n):
                dve.wait_ge(sm["lru_hi"], at(n + 1))
                h, l = sets[2]
                c = slice(TOK * n, TOK * (n + 1))
                V.tensor_tensor(l[:, c], scan[:, 0:TOK], h[:, c].bitcast(f32), ALU.subtract)\
                    .then_inc(sm["lru_lo"], 1)

            def lambda_sums():
                dve.wait_ge(sm["con_in"], 16)
                dve.wait_ge(sm["row_in"], 16)
                dve.wait_ge(sm["par_in"], 16)
                for i in range(2):
                    a = row[:, RLAM + 2 * DK * i:RLAM + 2 * DK * i + DK]
                    b = row[:, RLAM + 2 * DK * i + DK:RLAM + 2 * DK * (i + 1)]
                    ins = V.tensor_tensor(ob[:, DK * i:DK * (i + 1)], a, b, ALU.mult)
                link(ins)
                V.tensor_reduce(lamv[:, 0:2], ob[:, 0:2 * DK].rearrange("p (n d) -> p n d", d=DK), AX.X, ALU.add)
                lam = par[:, PCOL["lam"]:PCOL["lam"] + 2 * LB]
                w = 2 * LB
                link(V.tensor_scalar(head_gain, par[:, PCOL["subln"]:PCOL["subln"] + 1],
                                     1.0 - LAM_INIT, None, ALU.mult))
                link(V.tensor_scalar(lruc[:, 0:w], lam, -1.0, None, ALU.mult))
                V.tensor_tensor(lruc[:, 0:w], lruc[:, 0:w], lam, ALU.max).then_inc(sm["lamx_ok"], 1)

            def lambda_done():
                dve.wait_ge(sm["lame_ok"], 1)
                link(V.tensor_tensor(lamv[:, 2:3], lamv[:, 3:4], lamv[:, 2:3], ALU.subtract))
                link(V.tensor_scalar(lamv[:, 2:3], lamv[:, 2:3], -LAM_INIT, None, ALU.add))

            def softplus(part):
                lam = par[:, PCOL["lam"]:PCOL["lam"] + 2 * LB]
                w = 2 * LB
                e, s, s2, pl = lruc[:, 3 * w:4 * w], lruc[:, 2 * w:3 * w], lruc[:, w:2 * w], lruc[:, 0:w]
                if part == 0:
                    dve.wait_ge(sm["lexp_ok"], 1)
                    link(V.tensor_scalar(s, e, 2.0, None, ALU.add))
                    link(V.reciprocal(s, s))
                    link(V.tensor_tensor(s, e, s, ALU.mult))
                    link(V.tensor_tensor(s2, s, s, ALU.mult))
                    link(V.tensor_scalar(pl, s2, 1.0 / 19, 1.0 / 17, ALU.mult, ALU.add))
                for k in ((15, 13, 11, 9), (7, 5, 3, 1))[part]:
                    link(V.tensor_tensor(pl, pl, s2, ALU.mult))
                    link(V.tensor_scalar(pl, pl, 1.0 / k, None, ALU.add))
                if part == 0:
                    return
                link(V.tensor_tensor(pl, pl, s, ALU.mult))
                link(V.tensor_scalar(s, lam, -1.0, 0.0, ALU.mult, ALU.max))
                link(V.scalar_tensor_tensor(out=pl, in0=pl, scalar=2.0, in1=s, op0=ALU.mult, op1=ALU.add))
                link(V.tensor_scalar(pl, pl, LRU_C / 2, None, ALU.mult))
                V.tensor_scalar(lruc[:, w:2 * w], pl, -1.0, None, ALU.mult)
                V.tensor_scalar(lruc[:, 2 * w:3 * w], par[:, PCOL["br"]:PCOL["br"] + w], 0.5, None, ALU.mult)
                V.tensor_scalar(lruc[:, 3 * w:4 * w], par[:, PCOL["bi"]:PCOL["bi"] + w], 0.5, None, ALU.mult)\
                    .then_inc(sm["lruc_ok"], 1)
                dve.wait_ge(sm["lruc_ok"], 1)

            def epi_last(g, i):
                if i == 0:
                    dve.wait_ge(sm["post_in"], 16)
                dve.wait_ge(sm["ysq_ok"], i + 1)
                a, done = acc_of(g)
                for b in range(TB):
                    ins = V.tensor_tensor(y[:, D * b + GW * i:D * b + GW * (i + 1)], a[:, GW * b:GW * (b + 1)],
                                          gpost[:, GW * i:GW * (i + 1)], ALU.mult)
                ins.then_inc(done, 1)

            steps = dict(lambda_sums=lambda_sums, lambda_done=lambda_done, softplus=softplus,
                         epi_add=epi_add, epi_relu2=epi_relu2, epi_stage=None, epi_silu=epi_silu,
                         epi_sigm=epi_sigm, epi_proj_a=epi_proj_a, epi_proj_b=epi_proj_b, x_rstd=x_rstd,
                         tail=tail, norm_sum=norm_sum, norm_root=norm_root, norm_scale=norm_scale,
                         norm_rope=norm_rope,
                         rope2=rope2, att_smx=att_smx, att_prob=att_prob, att_o=att_o, att_lo=att_lo,
                         pool_lo=pool_lo, lru_const=lru_const, conv=conv,
                         lru_square=lru_square, lru=lru, lru_lo=lru_lo,
                         epi_memk=None, epi_memv=None, epi_store=None, epi_store2=None, epi_last=epi_last)

            def run(slab):
                for name, args in sc.steps["dve"].get(slab, ()):
                    if steps[name]:
                        steps[name](*args)

            dve.wait_ge(sm["par_in"], 16)
            run(-1)
            for kind, g, info in segments():
                if kind == "group":
                    for s in range(S):
                        lo(N(g), s)
                        run(S * g + s)
                else:
                    with dve.Fori(0, NCHUNK - 1) as c:
                        cc = N(0, 1, c)
                        for k in range(8):
                            for s in range(S):
                                lo(cc * 8 + (g + k), s)
                                q = cc * 4 + (info["staged0"] + k)
                                t = cc * 4 + (info["tail0"] + k)
                                if s == 1 and k < 4:
                                    epi_relu2(cc * 8 + (g + k - 1), info["rst"], q, t)
                                if s == 5 and k < 4:
                                    tail(t, 1, 4 * k, None)
                                if s == 1 and k >= 4:
                                    a, done = acc_of(cc * 8 + (g + k - 1))
                                    xs = tokens(x, GW * (k - 4), GW, D)
                                    V.tensor_tensor(xs, two(a), xs, ALU.add).then_inc(done, 1)
            run(S * GALL + 1)
            dve.wait_ge(*gout(GALL - 1))
            link(V.tensor_reduce(fin_rs, fin_ss.rearrange("p (b n) -> p b n", b=TB), AX.X, ALU.add))
            link(rms(fin_rs, fin_rs, D, TB))
            dve.wait_ge(sm["x_again"], 16)
            for i in range(2 * TB):
                b, c = i // 2, slice(D // 2 * i, D // 2 * (i + 1))
                V.scalar_tensor_tensor(out=y[:, c], in0=y[:, c], scalar=fin_rs[:, b:b + 1], in1=x[:, c],
                                       op0=ALU.mult, op1=ALU.add).then_inc(sm["fin_ok"], 1)

        @block.tensor
        def _(pe):
            T = nc.tensor

            def slab(g, s, src, order):
                pe.wait_ge(w_lo, at(g * S + (s + 1)))
                a = acc[g.base % 2]
                if s == 0:
                    if g.base >= 2:
                        pe.wait_ge(out_of[g.base % 2], at(g.half()))
                h, l = sets[src]
                for t in range(SLAB_K):
                    kt = order[s] * SLAB_K + t
                    c = slice((s % RAW) * SLAB + GW * t, (s % RAW) * SLAB + GW * (t + 1))
                    for b in range(TB):
                        tok = slice(TOK * kt + P * b, TOK * kt + P * (b + 1))
                        first, last = s == 0 and t == 0, s == S - 1 and t == SLAB_K - 1
                        o = a[:, GW * b:GW * (b + 1)]
                        T.matmul(o, h[:, tok], whi[:, c], start=first, stop=False)
                        T.matmul(o, h[:, tok], wlo[:, c], start=False, stop=False)
                        ins = T.matmul(o, l[:, tok], whi[:, c], start=False, stop=last)
                ins.then_inc(mm, 1)

            def tail(t, src):
                t = t if isinstance(t, N) else N(t)
                source_ready(pe, src)
                if at_least_one(t):
                    pe.wait_ge(sm["tail_lo"], at(t))
                for j in range(4):
                    for b in range(TB):
                        o = TOK * j + P * b
                        ins = T.transpose(tp[:, o:o + P], source_tile(src, j, b), ident)
                ins.then_inc(sm["tail_tp"], 1)

            def mk_tp(l):
                pe.wait_ge(sm["mk_norm"], at(l + 1))
                if l:
                    pe.wait_ge(sm["att_o"], MEM1J - 1)
                for h in range(MH):
                    for b in range(TB):
                        o = TOK * h + P * b
                        ins = T.transpose(sd[:, o:o + P], mkv[:, GW * b + MD * h:][:, 0:MD], ident)
                ins.then_inc(sm["mk_tp"], 1)

            def att_in(j):
                if row_jobs(j):
                    pe.wait_ge(sm["att_lo"], at(row_jobs(j)))
                if is_dif(j):
                    h = j - DIFJ
                    pe.wait_ge(sm["pool_lo"], len(WINDOWS))
                    if h >= 2:
                        pe.wait_ge(sm["att_o"], at(j - 1))
                    if h in (1, DH - 1):
                        pe.wait_ge(sm["tail_lo"], sc.info["head_tail"] + (2 if h > 1 else 0))
                    pe.wait_ge(sm["q_norm"], 3)
                    pe.wait_ge(sm["k_norm"], at(h // 4 + 1))
                    for m in range(2):
                        for b in range(TB):
                            cq = D * b + QKW * m + DK * h
                            ck = 2 * POOLW * b + QKW * m + DK * h
                            o = (2 * m + b) * P
                            T.transpose(side(j)[0:DK, o:o + P], u[:, cq:cq + DK], ident)
                            ins = T.transpose(side(j)[0:DK, 4 * P + o:5 * P + o], kv[:, ck:ck + DK], ident)
                elif j < B2J:
                    l = j >= DIFJ
                    if l:
                        pe.wait_ge(sm["att_o"], MEM1J - 1)
                    pe.wait_ge(sm["mk_t"], at(l + 1))
                    pe.wait_ge(sm["mq_norm"], at(l + 1))
                    for h in range(2):
                        for b in range(TB):
                            c = D * b + POOLW + MD * (2 * (j % 2) + h)
                            ins = T.transpose(sd[:, (2 * h + b) * P:(2 * h + b + 1) * P], u[:, c:c + MD], ident)
                else:
                    i = j - B2J
                    pe.wait_ge(sm["rope"], 5)
                    for h in range(2):
                        for b in range(TB):
                            c = D * b + HD2 * (2 * i + h)
                            T.transpose(sd[:, (2 * h + b) * P:(2 * h + b + 1) * P], u[:, c:c + HD2], ident)
                    for b in range(TB):
                        c = GW * b + HD2 * (i // 2)
                        ins = T.transpose(sd[:, (4 + b) * P:(5 + b) * P], mkv[:, c:c + HD2], ident)
                ins.then_inc(sm["att_in"], 1)

            def att_score(j):
                pe.wait_ge(sm["att_qk"], at(j + 1))
                q = qk_of(j)
                for r in range(4):
                    o = scores(side(j), j, r)
                    if is_dif(j):
                        kc = 4 * P + 2 * P * (r // 2)
                        ins = T.matmul(o, q[0:DK, P * r:P * (r + 1)], q[0:DK, kc:kc + P * (r % 2 + 1)],
                                       start=True, stop=True)
                    elif j < B2J:
                        kt = (2 * (j % 2) + r // 2) * TOK
                        ins = T.matmul(o, q[:, P * r:P * (r + 1)], mkv[:, kt:kt + TOK], start=True, stop=True)
                    else:
                        ins = T.matmul(o, q[:, P * r:P * (r + 1)], q[:, 4 * P:6 * P], start=True, stop=True)
                ins.then_inc(sm["att_score"], 1)

            def att_pt(j):
                pe.wait_ge(sm["att_prob"], at(j + 1))
                for o in range(3 if is_dif(j) else 8):
                    ins = T.transpose(side(j)[:, P * o:P * (o + 1)], prob_of(j)[:, P * o:P * (o + 1)], ident)
                ins.then_inc(sm["att_pt"], 1)

            def att_pv(j):
                pe.wait_ge(sm["att_ptc"], at(j + 1))
                if is_dif(j):
                    s, n = gout(sc.info["kv"][2 * ((j - DIFJ) // 4) + 1])
                elif j < B2J:
                    s, n = gout(sc.info["mem"][j >= DIFJ] + 1)
                else:
                    s, n = gout(sc.info["k2"] + 1)
                pe.wait_ge(s, n)
                if is_dif(j):
                    for b, k, first, last in ((0, 0, True, True), (1, 0, True, False), (1, 1, False, True)):
                        c = 2 * POOLW * k + 2 * QKW + DV * (j - DIFJ)
                        o = P * (b + k)
                        ins = T.matmul(side(j)[:, P * b:P * (b + 1)], qk_of(j)[:, o:o + P], kv[:, c:c + DV],
                                       start=first, stop=last)
                    ins.then_inc(sm["att_pv"], 1)
                    return
                for r in range(4):
                    for k in range(2):
                        if j < B2J:
                            c = 2 * GW + GW * k + MD * (2 * (j % 2) + r // 2)
                        else:
                            c = 2 * GW + GW * k + HD2 * ((j - B2J) // 2)
                        ins = T.matmul(sd[:, P * r:P * (r + 1)], qk[:, (2 * r + k) * P:(2 * r + k + 1) * P],
                                       mkv[:, c:c + P], start=k == 0, stop=k == 1)
                ins.then_inc(sm["att_pv"], 1)

            def att_ot(j):
                pe.wait_ge(sm["att_o"], at(j + 1))
                for r in range(4):
                    ins = T.transpose(sd[:, P * r:P * (r + 1)], ob[:, P * r:P * (r + 1)], ident)
                ins.then_inc(sm["att_ot"], 1)

            def pool_mix(i, g):
                pe.wait_ge(sm["att_lo"], MEMJ + 2)
                if i:
                    pe.wait_ge(sm["pool_lo"], i)
                pe.wait_ge(sm["pm_in"], 16)
                s, n = gout(g)
                pe.wait_ge(s, n)
                s, n = gout(g - 1)
                pe.wait_ge(s, n)
                for t in range(PGT):
                    for b in range(TB):
                        c = D * b + PG * i + P * t
                        m = (TB * i + b) * TOK
                        ins = T.matmul(sd[:, TOK * t:TOK * (t + 1)], u[:, c:c + P], poolm[:, m:m + TOK],
                                       start=b == 0, stop=b == TB - 1)
                ins.then_inc(sm["pool_mix"], 1)

            def pool_mm(i):
                pe.wait_ge(sm["pool_mid"], at(i + 1))
                pe.wait_ge(sm[f"pw{i % 2}_in"], at(16 * (i // 2 + 1)))
                w = pw[:, (i % 2) * PGT * PG:(i % 2 + 1) * PGT * PG]
                for o in range(PGT):
                    for k in range(PGT):
                        ins = T.matmul(sd[:, TOK * o:TOK * (o + 1)], w[:, PG * k + P * o:PG * k + P * (o + 1)],
                                       qk[:, TOK * k:TOK * (k + 1)], start=k == 0, stop=k == PGT - 1)
                ins.then_inc(sm["pool_mm"], 1)

            def gates(n):
                pe.wait_ge(sm["conv_ok"], at(n + 1))
                if n:
                    pe.wait_ge(sm["gates_ok"], at(n))
                pe.wait_ge(sm["att_lo"], row_jobs(NJOB))
                pe.wait_ge(sm[f"lw{n % 2}_in"], at(32 * (n // 2 + 1)))
                for d in range(2):
                    for k in range(2):
                        o = 2 * d + k
                        w = lw[:, ((n % 2) * 4 + o) * P:((n % 2) * 4 + o + 1) * P]
                        ins = T.matmul(sd[:, TOK * o:TOK * (o + 1)], w, xhs[:, TOK * (n % 2):TOK * (n % 2 + 1)],
                                       start=True, stop=True)
                ins.then_inc(sm["gates_pe"], 1)

            steps = dict(tail=tail, mk_tp=mk_tp, att_in=att_in, att_score=att_score, att_pt=att_pt,
                         att_pv=att_pv, att_ot=att_ot, pool_mix=pool_mix, pool_mm=pool_mm, gates=gates)

            def run(slab):
                for name, args in sc.steps["pe"].get(slab, ()):
                    steps[name](*args)

            pe.wait_ge(sm["ident_in"], 16)
            run(-1)
            for kind, g, info in segments():
                if kind == "group":
                    for s in range(S):
                        for name, count in info.need.get(s, ()):
                            pe.wait_ge(sm[name], at(count))
                        slab(N(g), s, info.src, info.order)
                        run(S * g + s)
                else:
                    order = list(range(S))
                    with pe.Fori(0, NCHUNK - 1) as c:
                        cc = N(0, 1, c)
                        for k, (w, r, col, src) in enumerate(loop_groups(info, cc)):
                            for s in range(S):
                                if k == 3 and s in (0, S - 2):
                                    pe.wait_ge(sm["tail_lo"], at(cc * 4 + (info["tail0"] + (3 if s == 0 else 4))))
                                slab(cc * 8 + (g + k), s, src, order)
                                if s == 3 and k < 4:
                                    tail(cc * 4 + (info["tail0"] + k), ("staged", cc * 4 + (info["staged0"] + k)))


def constants():
    f = np.float32
    const = np.zeros((P, NCON), f)
    const[:, CID:CID + P] = np.eye(P, dtype=f)
    tok = np.arange(TOK)
    q = (np.arange(P)[:, None, None] + P * np.arange(TB)[None, :, None])
    key = tok[None, None, :]
    causal = np.where(key <= q, f(0), f(-1e30))
    const[:, CCAUS:CCAUS + 3 * P] = np.concatenate([causal[:, 0, 0:P], causal[:, 1]], axis=1)
    const[:, CBAND:CBAND + 2 * TOK] = np.where(np.abs(key - q) <= 128, f(0), f(-1e30)).reshape(P, -1)
    for col, half in ((CR1, ROPE1), (CR2, ROPE2)):
        inv = (f(THETA) ** (-(np.arange(half, dtype=f) * f(2)) / f(2 * half))).astype(f)
        ang = (tok.astype(f)[:, None] * inv[None, :]).astype(f).astype(np.float64)
        cs = np.stack([np.cos(ang), np.sin(ang)]).astype(f)
        cs = cs.reshape(2, TB, P, half).transpose(2, 0, 1, 3)
        const[:, col:col + 2 * TB * half] = cs.reshape(P, -1)
    pm = np.zeros((len(WINDOWS), TOK, TOK), f)
    for i, w in enumerate(WINDOWS):
        src, dst = tok[:, None], tok[None, :]
        pm[i] = np.where((src <= dst) & (src > dst - w), f(1) / np.minimum(dst + 1, w).astype(f), f(0))
        pm[i] -= np.eye(TOK, dtype=f)
    pm = pm.reshape(len(WINDOWS), TB, P, TOK).transpose(2, 0, 1, 3).reshape(P, -1)
    return const, np.ascontiguousarray(pm)


def packed(inputs):
    def tiles(a):
        return np.asarray(a).reshape(-1, P).T

    cols = {"mix0": tiles(inputs["mix_norm"][0]), "mix1": tiles(inputs["mix_norm"][1]),
            "ffn0": tiles(inputs["ffn_norm"][0]), "ffn1": tiles(inputs["ffn_norm"][1]),
            "kv": tiles(inputs["kv_norm"]), "mem0": tiles(inputs["mem_norm"][0]),
            "mem1": tiles(inputs["mem_norm"][1]), "pre": tiles(inputs["norm_pre_w_2"][0]),
            "mq0": tiles(inputs["mem_q_norm"][0]), "mq1": tiles(inputs["mem_q_norm"][1]),
            "mk0": tiles(inputs["mem_k_norm"][0]), "mk1": tiles(inputs["mem_k_norm"][1]),
            "subln": tiles(inputs["subln_norm"][0]), "pscale": tiles(inputs["pool_scale"][0]),
            "convw": np.asarray(inputs["conv_w_2"][0]).reshape(4, LB, P).transpose(2, 1, 0).reshape(P, -1),
            "convb": tiles(inputs["conv_b_2"][0]),
            "br": tiles(inputs["lru_b_r_2"][0]), "bi": tiles(inputs["lru_b_i_2"][0]),
            "lam": tiles(inputs["lru_lambda_2"][0])}
    par = np.concatenate([cols[n] for n in PCOL], axis=1)
    row = np.concatenate([np.asarray(inputs["k_norm"]), np.asarray(inputs["q_norm"][0]),
                          np.asarray(inputs["attn_sink_2"][0]), np.asarray(inputs["diff_lambda"][0]).reshape(-1)])
    return np.ascontiguousarray(par), np.tile(row[None, :], (P, 1))


def kernel(**inputs):
    import concourse.bacc as bacc
    from concourse.bass_utils import run_bass_kernel_spmd

    inputs = {n: np.asarray(a) for n, a in inputs.items()}
    const, poolm = constants()
    par, row = packed(inputs)
    arrays = {n: inputs[n] for n in ("x", "mem", "w_in", "w_out", "w_mem_kv", "w_ff1", "w_ff2", "pool_w", "w_kv",
                                     "w_in_2", "lru_w_r_2", "lru_w_i_2", "w_proj_a_2", "w_proj_b_2",
                                     "w_out_2")}
    arrays.update(const=const, poolm=poolm, par=par, row=row,
                  post=np.tile(inputs["norm_post_w_2"][0][None, :], (P, 1)))
    nc = bacc.Bacc("TRN2", target_bir_lowering=False, num_devices=1)
    args, sent = {}, {}
    for n, a in arrays.items():
        sent["in_" + n] = np.ascontiguousarray(a)
        args[n] = nc.dram_tensor("in_" + n, a.shape, mybir.dt.from_np(a.dtype), kind="ExternalInput").ap()
    out = nc.dram_tensor("out", (1, TOK, D), mybir.dt.float32, kind="ExternalOutput").ap()
    build(nc, args, out)
    return run_bass_kernel_spmd(nc, [sent], core_ids=[0]).results[0]["out"]
```
